# Optimizing a Trainium2 kernel written in Bass

```python
import math
import jax, jax.numpy as jnp
from jax import lax
import numpy as np

D_MODEL = 1024
BATCH = 1
SEQ = 512
DEPTH = 2

HEAD_DIM = 64
FOX_HEADS = 8
DIFF_HEADS = 4
DIFF_VDIM = 2 * HEAD_DIM
Q_BLOCK = 128
ROPE_THETA = 10000.0
FOX_W = FOX_HEADS * HEAD_DIM
DIFF_QK_W = DIFF_HEADS * 2 * HEAD_DIM
DIFF_V_W = DIFF_HEADS * DIFF_VDIM
ATTN_IN_W = 3 * FOX_W + FOX_HEADS + 2 * DIFF_QK_W + DIFF_V_W
ATTN_CAT_W = FOX_W + DIFF_V_W
SSM_D_INNER = 2 * D_MODEL
SSM_HEAD_DIM = 64
SSM_HEADS = SSM_D_INNER // SSM_HEAD_DIM
SSM_GROUPS = 8
SSM_STATE = 128
SSM_CONV = 4
SSM_CHUNK = 128
SSM_CONV_DIM = SSM_D_INNER + 2 * SSM_GROUPS * SSM_STATE
SSM_IN_W = SSM_D_INNER + SSM_CONV_DIM + SSM_HEADS
D_FF = ((-(-8 * D_MODEL // 3)) + 255) // 256 * 256
NORM_EPS = 1e-6
GATED_NORM_EPS = 1e-5
N_ATTN_LAYERS = (DEPTH + 1) // 2
N_SSM_LAYERS = DEPTH // 2

kernel_name = "fox_diff_mamba2_hybrid_trunk"

def _rmsnorm(x, g, eps=NORM_EPS):
    xf = x.astype(jnp.float32)
    y = xf * lax.rsqrt(jnp.mean(xf * xf, axis=-1, keepdims=True) + eps)
    return (y * g.astype(jnp.float32)).astype(x.dtype)

def _rope(t, positions):
    d = t.shape[-1]
    inv = ROPE_THETA ** (-jnp.arange(0, d, 2, dtype=jnp.float32) / d)
    ang = positions.astype(jnp.float32)[:, None] * inv[None, :]
    cos, sin = jnp.cos(ang), jnp.sin(ang)
    tf = t.astype(jnp.float32)
    t1, t2 = tf[..., : d // 2], tf[..., d // 2:]
    return jnp.concatenate([t1 * cos - t2 * sin, t2 * cos + t1 * sin], axis=-1).astype(t.dtype)

def _split_blocks(t, axis):
    s = t.shape
    t = t.reshape(s[:axis] + (s[axis] // Q_BLOCK, Q_BLOCK) + s[axis + 1:])
    return jnp.moveaxis(t, axis, 0)

def _merge_blocks(t, axis):
    t = jnp.moveaxis(t, 0, axis)
    s = t.shape
    return t.reshape(s[:axis] + (s[axis] * s[axis + 1],) + s[axis + 2:])

def _fox_attention(q, k, v, log_f):
    S = q.shape[2]
    scale = HEAD_DIM ** -0.5
    cum = jnp.cumsum(log_f, axis=-1)
    kpos = jnp.arange(S)
    starts = jnp.arange(S // Q_BLOCK) * Q_BLOCK

    def body(args):
        q_blk, cum_blk, start = args
        s = jnp.einsum('bhqd,bhkd->bhqk', q_blk, k).astype(jnp.float32) * scale
        s = s + cum_blk[..., :, None] - cum[..., None, :]
        qpos = start + jnp.arange(Q_BLOCK)
        s = jnp.where(kpos[None, :] <= qpos[:, None], s, -jnp.inf)
        p = jax.nn.softmax(s, axis=-1).astype(v.dtype)
        return jnp.einsum('bhqk,bhkd->bhqd', p, v)

    out = lax.map(body, (_split_blocks(q, 2), _split_blocks(cum, 2), starts))
    return _merge_blocks(out, 2)

def _diff_attention(q, k, v, lam):
    S = q.shape[3]
    scale = HEAD_DIM ** -0.5
    kpos = jnp.arange(S)
    starts = jnp.arange(S // Q_BLOCK) * Q_BLOCK

    def body(args):
        q_blk, start = args
        s = jnp.einsum('bhcqd,bhckd->bhcqk', q_blk, k).astype(jnp.float32) * scale
        qpos = start + jnp.arange(Q_BLOCK)
        s = jnp.where(kpos[None, :] <= qpos[:, None], s, -jnp.inf)
        p = jax.nn.softmax(s, axis=-1)
        w = (p[:, :, 0] - lam * p[:, :, 1]).astype(v.dtype)
        return jnp.einsum('bhqk,bhkd->bhqd', w, v)

    out = lax.map(body, (_split_blocks(q, 3), starts))
    return _merge_blocks(out, 2)

def _attn_mixer(h, w_in, b_forget, w_out, lam_params, subln, layer_idx):
    Bsz, S, _ = h.shape
    proj = h @ w_in
    cuts = np.cumsum([FOX_W, FOX_W, FOX_W, FOX_HEADS, DIFF_QK_W, DIFF_QK_W]).tolist()
    fq, fk, fv, ff, dq, dk, dv = jnp.split(proj, cuts, axis=-1)

    def heads(t, n, d):
        return t.reshape(Bsz, S, n, d).transpose(0, 2, 1, 3)

    log_f = jax.nn.log_sigmoid((ff + b_forget).astype(jnp.float32)).transpose(0, 2, 1)
    y_fox = _fox_attention(heads(fq, FOX_HEADS, HEAD_DIM), heads(fk, FOX_HEADS, HEAD_DIM),
                           heads(fv, FOX_HEADS, HEAD_DIM), log_f)

    positions = jnp.arange(S)
    dq = _rope(dq.reshape(Bsz, S, DIFF_HEADS, 2, HEAD_DIM).transpose(0, 2, 3, 1, 4), positions)
    dk = _rope(dk.reshape(Bsz, S, DIFF_HEADS, 2, HEAD_DIM).transpose(0, 2, 3, 1, 4), positions)
    lam_init = 0.8 - 0.6 * math.exp(-0.3 * layer_idx)
    lp = lam_params.astype(jnp.float32)
    lam = jnp.exp(jnp.sum(lp[0] * lp[1])) - jnp.exp(jnp.sum(lp[2] * lp[3])) + lam_init
    y_diff = _diff_attention(dq, dk, heads(dv, DIFF_HEADS, DIFF_VDIM), lam)
    y_diff = _rmsnorm(y_diff, subln) * (1.0 - lam_init)

    y = jnp.concatenate([y_fox.transpose(0, 2, 1, 3).reshape(Bsz, S, FOX_W),
                         y_diff.transpose(0, 2, 1, 3).reshape(Bsz, S, DIFF_V_W)], axis=-1)
    return y @ w_out

def _causal_dwconv(u, w, b):
    K = w.shape[0]
    out = lax.conv_general_dilated(u, w[:, None, :].astype(u.dtype), window_strides=(1,),
                                   padding=[(K - 1, 0)], dimension_numbers=('NWC', 'WIO', 'NWC'),
                                   feature_group_count=u.shape[-1])
    return out + b

def _ssd_scan(x, dt, A, Bm, Cm):
    b, S, H, P = x.shape
    G, N = Bm.shape[2], Bm.shape[3]
    R, c, L = H // G, S // SSM_CHUNK, SSM_CHUNK
    X = (x.astype(jnp.float32) * dt[..., None]).reshape(b, c, L, G, R, P)
    Bc = Bm.astype(jnp.float32).reshape(b, c, L, G, N)
    Cc = Cm.astype(jnp.float32).reshape(b, c, L, G, N)
    Adt = (dt * A).reshape(b, c, L, G, R).transpose(0, 3, 4, 1, 2)
    Acs = jnp.cumsum(Adt, axis=-1)
    causal = jnp.tril(jnp.ones((L, L), dtype=bool))
    Lmat = jnp.exp(jnp.where(causal, Acs[..., :, None] - Acs[..., None, :], -jnp.inf))
    CB = jnp.einsum('bclgn,bcsgn->bgcls', Cc, Bc)
    y_diag = jnp.einsum('bgrcls,bcsgrp->bclgrp', CB[:, :, None] * Lmat, X)
    decay_states = jnp.exp(Acs[..., -1:] - Acs)
    states = jnp.einsum('bcsgn,bgrcs,bcsgrp->bcgrpn', Bc, decay_states, X)
    chunk_decay = jnp.exp(Acs[..., -1])

    def step(state, inp):
        s_c, dec = inp
        return state * dec[..., None, None] + s_c, state

    init = jnp.zeros((b, G, R, P, N), jnp.float32)
    _, prev = lax.scan(step, init, (jnp.moveaxis(states, 1, 0), jnp.moveaxis(chunk_decay, 3, 0)))
    y_off = jnp.einsum('bclgn,cbgrpn,bgrcl->bclgrp', Cc, prev, jnp.exp(Acs))
    return (y_diag + y_off).reshape(b, S, H, P)

def _ssd_mixer(h, w_in, conv_w, conv_b, dt_bias, a_log, d_skip, norm_w, w_out):
    Bsz, S, _ = h.shape
    zxbcdt = h @ w_in
    z, xbc, dt = jnp.split(zxbcdt, [SSM_D_INNER, SSM_D_INNER + SSM_CONV_DIM], axis=-1)
    xbc = jax.nn.silu(_causal_dwconv(xbc, conv_w, conv_b))
    xs, Bm, Cm = jnp.split(xbc, [SSM_D_INNER, SSM_D_INNER + SSM_GROUPS * SSM_STATE], axis=-1)
    xs = xs.reshape(Bsz, S, SSM_HEADS, SSM_HEAD_DIM)
    Bm = Bm.reshape(Bsz, S, SSM_GROUPS, SSM_STATE)
    Cm = Cm.reshape(Bsz, S, SSM_GROUPS, SSM_STATE)
    dt = jax.nn.softplus((dt + dt_bias).astype(jnp.float32))
    A = -jnp.exp(a_log.astype(jnp.float32))
    y = _ssd_scan(xs, dt, A, Bm, Cm)
    y = (y + d_skip.astype(jnp.float32)[:, None] * xs.astype(jnp.float32)).reshape(Bsz, S, SSM_D_INNER)
    g = (y * jax.nn.silu(z.astype(jnp.float32))).reshape(Bsz, S, SSM_GROUPS, -1)
    g = g * lax.rsqrt(jnp.mean(g * g, axis=-1, keepdims=True) + GATED_NORM_EPS)
    g = g.reshape(Bsz, S, SSM_D_INNER) * norm_w.astype(jnp.float32)
    return g.astype(h.dtype) @ w_out

def _swiglu(h, w_gate, w_up, w_down):
    return (jax.nn.silu(h @ w_gate) * (h @ w_up)) @ w_down

def setup_inputs(seed: int = 0) -> dict:
    key = jax.random.key(seed)
    k = jax.random.split(key, 20)
    nrm = jax.random.normal
    f32 = jnp.float32
    NA, NM = N_ATTN_LAYERS, N_SSM_LAYERS
    dt0 = jnp.exp(jax.random.uniform(k[11], (NM, SSM_HEADS), f32, math.log(1e-3), math.log(1e-1)))
    return {
        "x": nrm(k[0], (BATCH, SEQ, D_MODEL), f32),
        "norm_mix": 1.0 + 0.02 * nrm(k[1], (DEPTH, D_MODEL), f32),
        "norm_ffn": 1.0 + 0.02 * nrm(k[2], (DEPTH, D_MODEL), f32),
        "attn_w_in": nrm(k[3], (NA, D_MODEL, ATTN_IN_W), f32) * D_MODEL ** -0.5,
        "attn_b_forget": jax.random.uniform(k[4], (NA, FOX_HEADS), f32, 1.0, 4.0),
        "attn_w_out": nrm(k[5], (NA, ATTN_CAT_W, D_MODEL), f32) * ATTN_CAT_W ** -0.5,
        "diff_lambda": 0.1 * nrm(k[6], (NA, 4, HEAD_DIM), f32),
        "diff_subln": 1.0 + 0.02 * nrm(k[7], (NA, DIFF_VDIM), f32),
        "ssm_w_in": nrm(k[8], (NM, D_MODEL, SSM_IN_W), f32) * D_MODEL ** -0.5,
        "ssm_conv_w": nrm(k[9], (NM, SSM_CONV, SSM_CONV_DIM), f32) * SSM_CONV ** -0.5,
        "ssm_conv_b": 0.02 * nrm(k[10], (NM, SSM_CONV_DIM), f32),
        "ssm_dt_bias": dt0 + jnp.log(-jnp.expm1(-dt0)),
        "ssm_a_log": jnp.log(jax.random.uniform(k[12], (NM, SSM_HEADS), f32, 1.0, 16.0)),
        "ssm_d": 1.0 + 0.02 * nrm(k[13], (NM, SSM_HEADS), f32),
        "ssm_norm": 1.0 + 0.02 * nrm(k[14], (NM, SSM_D_INNER), f32),
        "ssm_w_out": nrm(k[15], (NM, SSM_D_INNER, D_MODEL), f32) * SSM_D_INNER ** -0.5,
        "ffn_w_gate": nrm(k[16], (DEPTH, D_MODEL, D_FF), f32) * D_MODEL ** -0.5,
        "ffn_w_up": nrm(k[17], (DEPTH, D_MODEL, D_FF), f32) * D_MODEL ** -0.5,
        "ffn_w_down": nrm(k[18], (DEPTH, D_FF, D_MODEL), f32) * D_FF ** -0.5,
        "final_norm": 1.0 + 0.02 * nrm(k[19], (D_MODEL,), f32),
    }

def reference(x, norm_mix, norm_ffn, attn_w_in, attn_b_forget, attn_w_out, diff_lambda, diff_subln,
              ssm_w_in, ssm_conv_w, ssm_conv_b, ssm_dt_bias, ssm_a_log, ssm_d, ssm_norm, ssm_w_out,
              ffn_w_gate, ffn_w_up, ffn_w_down, final_norm):
    for i in range(DEPTH):
        h = _rmsnorm(x, norm_mix[i])
        if i % 2 == 0:
            j = i // 2
            x = x + _attn_mixer(h, attn_w_in[j], attn_b_forget[j], attn_w_out[j],
                                diff_lambda[j], diff_subln[j], i)
        else:
            j = i // 2
            x = x + _ssd_mixer(h, ssm_w_in[j], ssm_conv_w[j], ssm_conv_b[j], ssm_dt_bias[j],
                               ssm_a_log[j], ssm_d[j], ssm_norm[j], ssm_w_out[j])
        x = x + _swiglu(_rmsnorm(x, norm_ffn[i]), ffn_w_gate[i], ffn_w_up[i], ffn_w_down[i])
    return _rmsnorm(x, final_norm)


_drawn_inputs = setup_inputs


def setup_inputs(seed=0):
    import zlib

    import numpy as np

    out = dict(_drawn_inputs(seed))
    spreads = {}
    factors = {'norm_ffn': 2.866,
     'diff_subln': 3.948,
     'ssm_conv_b': 3.219,
     'ssm_d': 6.618,
     'ssm_norm': 4.337,
     'final_norm': 2.839}
    for name, (base, spread) in spreads.items():
        noise = np.random.default_rng([zlib.crc32(name.encode()), seed]).standard_normal(out[name].shape)
        drawn = base * np.exp(spread * noise) if base else spread * noise
        out[name] = __import__('jax').numpy.asarray(drawn.astype(out[name].dtype))
    for name, factor in factors.items():
        out[name] = (out[name] * factor).astype(out[name].dtype)
    return out
```

```python
from contextlib import ExitStack
import math

import numpy as np

import concourse.bass as bass
from concourse import mybir

F32 = mybir.dt.float32
F32R = mybir.dt.float32r
ALU = mybir.AluOpType
ACT = mybir.ActivationFunctionType
AX = mybir.AxisListType

P = 128
SEQ = 512
DM = 1024
KC = DM // P
NQB = SEQ // P
HD = 64
FOX_HEADS = 8
UNITS = 4
DFF = 2816
FC = DFF // P
DI = 2048
GROUPS = 8
HPG = 4
SSM_HEADS = 32
DOWN_CUT = (8, 8, 6)
EPS = 1e-6
GATED_EPS = 1e-5
LAM_INIT = 0.8 - 0.6 * math.exp(-0.3 * 0)
NEG = -1e30
GPW = 4 * 5 + 4
LOG1P_TERMS = 8

T_ATTN, G_ATTN = 0, 0
T_AO, G_AO = T_ATTN + 6 * UNITS, G_ATTN + 6 * UNITS
T_GU = [T_AO + KC, None]
G_GU = [G_AO + KC, None]
T_DN = [T_GU[0] + 2 * FC, None]
G_DN = [G_GU[0] + 2 * FC, None]
T_SSM, G_SSM = T_DN[0] + 3 * KC, G_DN[0] + KC
T_SO, G_SO = T_SSM + 6 * GROUPS, G_SSM + 6 * GROUPS
T_GU[1], G_GU[1] = T_SO + 2 * KC, G_SO + KC
T_DN[1], G_DN[1] = T_GU[1] + 2 * FC, G_GU[1] + 2 * FC
T_ALL = T_DN[1] + 3 * KC
PRE, RES_AO, RES_DN0, RES_SO, RES_DN1 = 0, KC, 2 * KC, 3 * KC, 4 * KC


def columns(t, c, width=SEQ):
    return t[:, c * width:(c + 1) * width] if isinstance(c, int) else t[:, bass.ds(c * width, width)]


def width_at(t, at, n):
    return t[:, at:at + n] if isinstance(at, int) else t[:, bass.ds(at, n)]


def trunk(nc, xT, w_ff, w_attn, w_ao, w_gu, w_dn, w_dt, w_ssm, w_so, ssm_heads, ssm_params, gains, fox_cols, rope, lam, subln, outT):
    with ExitStack() as ctx:
        sems = {}

        def S(name):
            if name not in sems:
                sems[name] = ctx.enter_context(nc.semaphore(name))
            return sems[name]

        def sb(name, shape, dt=F32, stack=ctx):
            return stack.enter_context(nc.sbuf_tensor(name, shape, dt))

        x = sb("x", [P, KC * SEQ])
        hT = [sb("hT_hi", [P, KC * SEQ], F32R), sb("hT_lo", [P, KC * SEQ], F32R)]
        raw = [sb(f"w_raw{r}", [P, KC * P]) for r in range(2)]
        w_hi = [sb(f"w_hi{r}", [P, KC * P], F32R) for r in range(2)]
        w_lo = [sb(f"w_lo{r}", [P, KC * P], F32R) for r in range(2)]
        rb = sb("inv_rms", [P, SEQ])
        sq = sb("sq", [P, SEQ])
        acc = sb("sum_sq", [P, SEQ])
        ident = sb("ident", [P, P])
        ones = sb("ones", [P, P])
        gain = sb("gain", [P, 5 * KC])
        eps_c = sb("eps_c", [P, 2])
        causal = sb("causal", [P, P])
        last_row = sb("last_row", [P, P])
        gp = sb("ssm_params_sb", [P, GROUPS * GPW])
        hp = sb("ssm_heads_sb", [SSM_HEADS, 2])

        with ExitStack() as st:
            a = lambda name, shape, dt=F32: sb(name, shape, dt, st)
            ff_w = [a("ff_raw", [P, KC * P]), a("ff_hi", [P, KC * P], F32R), a("ff_lo", [P, KC * P], F32R)]
            ff_t = [a(f"ff_t{n}", [FOX_HEADS, SEQ]) for n in range(6)]
            ff_c = [a("ff_c_hi", [FOX_HEADS, SEQ], F32R), a("ff_c_lo", [FOX_HEADS, SEQ], F32R)]
        with ExitStack() as st:
            a = lambda name, shape, dt=F32: sb(name, shape, dt, st)
            yT = [a("yT_hi", [P, KC * SEQ], F32R), a("yT_lo", [P, KC * SEQ], F32R)]
            crow = a("fox_rows", [2, FOX_HEADS * SEQ], F32R)
            qs = {k: [a(f"{k}_q_{p}", [P, SEQ], F32R) for p in ("hi", "lo")] for k in "fd"}
            ks = {k: [a(f"{k}_k_{p}", [P, SEQ], F32R) for p in ("hi", "lo")] for k in "fd"}
            vs = {"f": [[a(f"f_v{m}_{p}", [P, NQB, P], F32R) for p in ("hi", "lo")] for m in range(2)]}
            vs["d"] = [[a(f"d_v_{p}", [P, NQB, P], F32R) for p in ("hi", "lo")]]
            vt = a("v_T", [P, SEQ])
            ev = [a(f"evac_{r}", [P, SEQ]) for r in "qk"]
            sw = a("swapped", [P, SEQ])
            rot = a("rotated", [P, SEQ])
            cos = a("cos", [P, SEQ])
            sin = a("sin", [P, SEQ])
            pr = [[a(f"p{par}{m}", [P, SEQ]) for m in range(2)] for par in range(2)]
            pt = [[a(f"pT{m}_{p}", [P, SEQ], F32R) for p in ("hi", "lo")] for m in range(2)]
            negmax = a("negmax", [P, 2, 2])
            rowsum = a("rowsum", [P, 2, 2])
            rinv = a("rinv", [P, 2, 2])
            dsq = a("d_sq", [P, SEQ])
            drs = a("d_rs", [P, SEQ])
            dy = a("d_y", [P, SEQ])
            ones2 = a("ones2", [2, P], F32R)
            ident_r = a("ident_r", [P, P], F32R)
            negmask = a("negmask", [P, P])
            negmask_r = a("negmask_r", [P, P], F32R)
            lamt = a("lam_t", [P, 4, HD])
            lamp = a("lam_p", [P, 2, HD])
            lams = a("lam_s", [P, 4])
            neglam = a("neglam", [P, 1])
            sublnw = a("subln_w", [P, 1])
            bff = a("b_forget", [FOX_HEADS, 1])
        with ExitStack() as st:
            a = lambda name, shape, dt=F32: sb(name, shape, dt, st)
            act = [a("act_hi", [P, FC * SEQ], F32R), a("act_lo", [P, FC * SEQ], F32R)]
            fz = a("ffn_z", [P, SEQ])
            ft = a("ffn_t", [P, SEQ])
            fs = a("ffn_silu", [P, SEQ])
            fu = a("ffn_up", [P, SEQ])
            fa = a("ffn_act", [P, SEQ])

        with ExitStack() as st:
            a = lambda name, shape, dt=F32: sb(name, shape, dt, st)
            a("below_dt", [P, 2 * FC * SEQ + 5 * SEQ])
            dt_w = [a("dt_raw", [P, KC * P]), a("dt_hi", [P, KC * P], F32R), a("dt_lo", [P, KC * P], F32R)]
        with ExitStack() as st:
            a = lambda name, shape, dt=F32: sb(name, shape, dt, st)
            dt_t = [a(f"dt_t{n}", [SSM_HEADS, SEQ]) for n in range(6)]
            acol = a("A_col", [SSM_HEADS, 1])
            acsT = a("acs_T", [P, NQB * SSM_HEADS])
            decT = a("dec_T", [P, NQB * SSM_HEADS])
        NH4 = NQB * SSM_HEADS
        with ExitStack() as st:
            a = lambda name, shape, dt=F32: sb(name, shape, dt, st)
            gT = a("gated_T", [P, 2 * GROUPS * SEQ])
            ub = [a(f"u{j}", [P, SEQ + 3]) for j in range(4)]
            xs = [a(f"xs{j}", [P, SEQ]) for j in range(4)]
            bc = [[a(f"{n}_{p}", [P, SEQ], F32R) for p in ("hi", "lo")] for n in ("B", "C")]
            zc = [a(f"z{t}", [P, SEQ]) for t in range(2)]
            tt = [a(f"tanh{t}", [P, SEQ]) for t in range(2)]
            ab = a("acs_rows", [P, HPG * SEQ])
            ea = [a(f"exp_acs{t}", [P, SEQ]) for t in range(2)]
            cbm = a("cb_masked", [P, SEQ])
            xst = a("x_dt", [P, NQB, 2 * P])
            xp = [[a(f"xp{r}_{p}", [P, NQB, P], F32R) for p in ("hi", "lo")] for r in range(HPG)]
            xd = [a(f"xd_{p}", [P, 3, 2 * P], F32R) for p in ("hi", "lo")]
            bt = [a(f"b_tok_{p}", [P, 3 * P], F32R) for p in ("hi", "lo")]
            mm_ = [[a(f"m{r}_{p}", [P, SEQ], F32R) for p in ("hi", "lo")] for r in range(2)]
            state = [a(f"state{c}", [P, 2 * P]) for c in range(2)]
            prev = [a(f"prev_{p}", [P, 3 * 2 * P], F32R) for p in ("hi", "lo")]
            rg = cbm
            nacs = a("neg_acs_T", [P, NH4])
            dtT = a("dt_T", [P, NH4])
            dsT = a("decay_to_end", [P, NH4])
            cdT = a("chunk_decay", [P, NH4])
        with ExitStack() as st:
            a = lambda name, shape, dt=F32: sb(name, shape, dt, st)
            a("under_gated_T", [P, 2 * GROUPS * SEQ])
            gs = [a(f"gated_{p}", [P, 2 * GROUPS * SEQ], F32R) for p in ("hi", "lo")]

        acs_dram = nc.dram_tensor("acs_dram", [SSM_HEADS, SEQ], F32, kind="Internal").ap()
        rows_dram = nc.dram_tensor("rows_dram", [2 * FOX_HEADS, SEQ], F32, kind="Internal").ap()
        bank = [ctx.enter_context(nc.psum_tensor(f"bank{b}", [P, SEQ], F32)) for b in range(8)]
        GB = bank[0:2]
        SB = bank[2:4]
        TB = bank[4:6]
        OB = bank[6]
        XB = bank[7]
        OTHER = {"f": "d", "d": "f"}

        block = ctx.enter_context(nc.Block())

        @block.sync
        def _(sp):
            for c in range(KC):
                sp.dma_start(columns(x, c), xT[c]).then_inc(S(f"x_in{c}"), 16)
            for dst, src in ((gain, gains), (sublnw, subln), (bff, fox_cols), (lamt, lam.partition_broadcast(P)),
                             (cos, rope[0]), (sin, rope[1]), (gp, ssm_params), (hp, ssm_heads)):
                sp.dma_start(dst[:], src).then_inc(S("small_in"), 16)
            sp.dma_start(ff_w[0][:], w_ff).then_inc(S("ff_in"), 16)

            def load(T, r, src, blocks=KC):
                sp.wait_ge(S("w_lo"), T + 1)
                sp.dma_start(raw[r][:, 0:blocks * P], src).then_inc(S(f"w_in{r}"), 16)

            with sp.Fori(0, UNITS) as i:
                for j in range(6):
                    load(T_ATTN + 6 * i + j, j % 2, w_attn[bass.ds((6 * i + j) * P, P), :])
            with sp.Fori(0, KC // 2) as i:
                for j in range(2):
                    load(T_AO + 2 * i + j, j, w_ao[bass.ds((2 * i + j) * P, P), :])
            def ffn_loads(l):
                with sp.Fori(0, FC) as i:
                    for j in range(2):
                        load(T_GU[l] + 2 * i + j, j, w_gu[l][bass.ds((2 * i + j) * P, P), :])
                if l == 0:
                    sp.wait_ge(S("x_add"), KC)
                    sp.dma_start(dt_w[0][:], w_dt).then_inc(S("dt_in"), 16)
                with sp.Fori(0, KC // 2) as i:
                    for j in range(6):
                        m, cut = j // 3, j % 3
                        load(T_DN[l] + 6 * i + j, j % 2,
                             w_dn[l][bass.ds((2 * i + m) * P, P), sum(DOWN_CUT[:cut]) * P:sum(DOWN_CUT[:cut + 1]) * P],
                             DOWN_CUT[cut])

            ffn_loads(0)
            def ssm_loads(g):
                for j in range(6):
                    load(T_SSM + 6 * g + j, j % 2, w_ssm[bass.ds((6 * g + j) * P, P), :])

            def acs_rows(g):
                sp.wait_ge(S("m_lo"), HPG * g + 1)
                src = acs_dram[bass.ds(HPG * g, HPG), :].rearrange("h n -> (h n)").partition_broadcast(P)
                sp.dma_start(ab[:], src).then_inc(S("ab_in"), 16)

            ssm_loads(0)
            sp.wait_ge(S("acs_stored"), 16)
            acs_rows(0)
            with sp.Fori(1, GROUPS) as g:
                ssm_loads(g)
                acs_rows(g)
            with sp.Fori(0, KC // 2) as i:
                for j in range(4):
                    load(T_SO + 4 * i + j, j % 2,
                         w_so[bass.ds((2 * i + j // 2) * P, P), (j % 2) * DM:(j % 2 + 1) * DM])
            ffn_loads(1)
            for c in range(KC):
                sp.wait_ge(S("y_out"), c + 1)
                sp.dma_start(outT[c], columns(x, c)).then_inc(S("stored"), 16)
            sp.wait_ge(S("stored"), 16 * KC)

        @block.gpsimd
        def _(pool):
            pool.nop().then_inc(S("w_lo"), 2)
            pool.memset(ident[:], 0.0).then_inc(S("c_set"), 1)
            pool.memset(ones[:], 1.0).then_inc(S("c_set"), 1)
            pool.memset(negmask[:], 0.0).then_inc(S("c_set"), 1)
            pool.wait_ge(S("c_set"), 3)
            pool.affine_select(out=ident[:], in_=ident[:], compare_op=ALU.not_equal, fill=1.0, base=0,
                               pattern=[[-1, P]], channel_multiplier=1).then_inc(S("consts"), 1)
            pool.affine_select(out=negmask[:], in_=negmask[:], compare_op=ALU.is_ge, fill=NEG, base=0,
                               pattern=[[-1, P]], channel_multiplier=1).then_inc(S("consts"), 1)
            for m in range(2):
                for part in range(2):
                    pool.memset(vs["f"][m][part][:, :, HD * (1 - m):HD * (2 - m)].bitcast(F32), 0.0)\
                        .then_inc(S("consts"), 1)
            pool.affine_select(out=causal[:], in_=ones[:], compare_op=ALU.is_ge, fill=0.0, base=0,
                               pattern=[[1, P]], channel_multiplier=-1).then_inc(S("consts"), 1)
            pool.affine_select(out=last_row[:], in_=ones[:], compare_op=ALU.is_ge, fill=0.0, base=1 - P,
                               pattern=[[0, P]], channel_multiplier=1).then_inc(S("consts"), 1)
            pool.wait_ge(S("ff_w_hi"), 1)
            pool.tensor_tensor(ff_w[2][:], ff_w[0][:], ff_w[1][:].bitcast(F32), ALU.subtract).then_inc(S("ff_w_lo"), 1)

            def lo_parts(start, end):
                with pool.Fori(start // 2, end // 2) as i:
                    for r in range(2):
                        pool.wait_ge(S("w_hi"), 2 * i + r + 1)
                        pool.tensor_tensor(w_lo[r][:], raw[r][:], w_hi[r][:].bitcast(F32), ALU.subtract)\
                            .then_inc(S("w_lo"), 1)

            lo_parts(0, T_DN[0])
            pool.wait_ge(S("dt_w_hi"), 1)
            pool.tensor_tensor(dt_w[2][:], dt_w[0][:], dt_w[1][:].bitcast(F32), ALU.subtract).then_inc(S("dt_w_lo"), 1)
            lo_parts(T_DN[0], T_ALL)

        @block.tensor
        def _(pe):
            def hilo(out, lhs, rhs, first, last, lcut, rcut):
                for n, (u, v) in enumerate(((0, 0), (0, 1), (1, 0))):
                    mm = pe.matmul(out, lcut(lhs[u]), rcut(rhs[v]), start=first and n == 0, stop=last and n == 2)
                return mm

            def wblocks(T, G, r, g, rhs, kcs, k0, n_all, rcut):
                if kcs[0] == 0:
                    pe.wait_ge(S("w_lo"), T + 3)
                    if k0 == 0:
                        pe.wait_ge(S("g_out"), G + 1)
                for kc in kcs:
                    mm = hilo(GB[g][:], (w_hi[r], w_lo[r]), rhs, k0 + kc == 0, k0 + kc == n_all - 1,
                              lambda t: t[:, kc * P:(kc + 1) * P], lambda t: rcut(t, k0 + kc))
                return mm

            chunk = columns

            def sum_squares(n):
                pe.wait_ge(S("sq_sum"), KC * (n + 1) + 1)
                pe.matmul(XB[:], ones[:], acc[:], start=True, stop=True).then_inc(S("ms"), 1)

            for name, credit in (("tile_done", 2), ("v_turned", 1), ("turned", 2), ("pv", 5), ("s", 9),
                                 ("y_diag", 1), ("y_off", 2), ("state_mm", 1), ("g_ms", 1),
                                 ("b_turned", 1)):
                pe.nop().then_inc(S(name), credit)
            pe.wait_ge(S("consts"), 8)
            pe.wait_ge(S("ff_w_lo"), 1)
            for kc in range(KC):
                pe.wait_ge(S("h_lo"), kc + 1)
                mm = hilo(OB[:], ff_w[1:3], hT, kc == 0, kc == KC - 1,
                          lambda t: t[:, kc * P:(kc + 1) * P], lambda t: columns(t, kc))
            mm.then_inc(S("ff_mm"), 1)
            sum_squares(0)

            def gemm(k, u, c):
                j = c // 4 + 3 * (k == "d")
                T = T_ATTN + 6 * u + j
                mm = wblocks(T, T, j % 2, j % 2, hT, [2 * (c % 4), 2 * (c % 4) + 1], 0, KC, chunk)
                if c % 4 == 3:
                    mm.then_inc(S("tile_done"), 1)

            def v_turn(k, u):
                n = 2 * u + (k == "d")
                pe.wait_ge(S("g_out"), 6 * u + 3 * (k == "d") + 3)
                pe.wait_ge(S("v_lo"), n + 1)
                if k == "d":
                    pe.wait_ge(S("d_ln"), u + 1)
                elif not isinstance(u, int):
                    pe.wait_ge(S("d_ln"), u)
                for b in range(NQB):
                    mm = pe.transpose(XB[:, b * P:(b + 1) * P], vt[:, b * P:(b + 1) * P], ident[:])
                mm.then_inc(S("v_turned"), 1)

            def scores(k, u, s):
                n, N = 2 * u + (k == "d"), (s + 1) * P
                if s == 0:
                    pe.wait_ge(S("q_lo"), n + 2)
                    pe.wait_ge(S("k_lo"), n + 2)
                for m in range(2):
                    pe.wait_ge(S("exp"), 8 * n + 2 * s + m + 1)
                    row = slice(HD * m, HD * m + HD)
                    out = SB[m][:, 0:N]
                    hilo(out, qs[k], ks[k], True, False,
                         lambda t: t[row, s * P:(s + 1) * P], lambda t: t[row, 0:N])
                    if k == "f":
                        if m == 0 and s == 0:
                            pe.wait_ge(S("crow_in"), 16)
                        pe.matmul(out, ones2[:], width_at(crow, (2 * u + m) * SEQ, N), start=False, stop=False)
                    pe.matmul(SB[m][:, s * P:N], ident_r[:], negmask_r[:], start=False, stop=True)\
                        .then_inc(S("s"), 1)

            def turn(k, u, s):
                n = 2 * u + (k == "d")
                pe.wait_ge(S("p"), 4 * n + s + 1)
                for m in range(2 if k == "f" else 1):
                    for b in range(s + 1):
                        mm = pe.transpose(TB[m][:, b * P:(b + 1) * P], pr[s % 2][m][:, b * P:(b + 1) * P], ident[:])
                mm.then_inc(S("turned"), 1)

            def pv(k, u, s):
                n = 2 * u + (k == "d")
                pe.wait_ge(S("pT_lo"), 4 * n + s + 1)
                if s == 0:
                    pe.wait_ge(S("v_lo"), n + 2)
                    pe.wait_ge(S("o_out"), n + 1)
                maps = 2 if k == "f" else 1
                for m in range(maps):
                    for b in range(s + 1):
                        mm = hilo(OB[:, s * P:(s + 1) * P], vs[k][m], pt[m], m == 0 and b == 0,
                                  m == maps - 1 and b == s,
                                  lambda t: t[:, b, :], lambda t: t[:, b * P:(b + 1) * P])
                mm.then_inc(S("pv"), 1)

            def sub_ms(u, v_loaded):
                pe.wait_ge(S("d_sq"), u + 1)
                pe.wait_ge(S("v_lo"), v_loaded)
                pe.matmul(XB[:], ones[:], dsq[:], start=True, stop=True).then_inc(S("d_ms"), 1)

            def section(att, proj):
                kg = iter(range(12))

                def g(n=2):
                    for _ in range(n if proj else 0):
                        gemm(*proj, next(kg))
                if att is None:
                    g(12)
                    pe.wait_ge(S("ln"), 1)
                    v_turn(*proj)
                    return
                g()
                scores(*att, 0)
                g()
                scores(*att, 1)
                turn(*att, 0)
                g()
                pv(*att, 0)
                if proj:
                    v_turn(*proj)
                scores(*att, 2)
                turn(*att, 1)
                g()
                pv(*att, 1)
                scores(*att, 3)
                turn(*att, 2)
                g()
                pv(*att, 2)
                turn(*att, 3)
                g()
                pv(*att, 3)
                if att[0] == "d":
                    sub_ms(att[1], 2 * att[1] + (4 if proj else 3))

            section(None, ("f", 0))
            with pe.Fori(0, UNITS - 1) as i:
                section(("f", i), ("d", i))
                section(("d", i), ("f", i + 1))
            section(("f", UNITS - 1), ("d", UNITS - 1))
            section(("d", UNITS - 1), None)

            pe.wait_ge(S("o_out"), 2 * UNITS + 1)
            pe.wait_ge(S("dy_lo"), UNITS + 1)
            with pe.Fori(0, KC // 2) as i:
                for j in range(2):
                    T, G = T_AO + 2 * i + j, G_AO + 2 * i + j
                    wblocks(T, G, j, j, yT, range(KC), 0, KC, chunk).then_inc(S("tile_done"), 1)
            sum_squares(1)

            def ffn(l, norm):
                with pe.Fori(0, FC) as i:
                    for j in range(2):
                        wblocks(T_GU[l] + 2 * i + j, G_GU[l] + 2 * i + j, j, j, hT, range(KC), 0, KC, chunk)\
                            .then_inc(S("tile_done"), 1)
                pe.wait_ge(S("act_lo"), FC * (l + 1))
                with pe.Fori(0, KC // 2) as i:
                    for j in range(6):
                        m, cut = j // 3, j % 3
                        wblocks(T_DN[l] + 6 * i + j, G_DN[l] + 2 * i + m, j % 2, m, act, range(DOWN_CUT[cut]),
                                sum(DOWN_CUT[:cut]), FC, chunk).then_inc(S("tile_done"), 1)
                sum_squares(norm)

            ffn(0, 2)

            CB, TR, STB, YD, YO, NX = SB[0], SB[1], TB[0], TB[1], OB, XB
            pe.wait_ge(S("dt_w_lo"), 1)
            for kc in range(KC):
                pe.wait_ge(S("h_lo"), 2 * KC + kc + 1)
                mm = hilo(CB[:], dt_w[1:3], hT, kc == 0, kc == KC - 1,
                          lambda t: t[:, kc * P:(kc + 1) * P], lambda t: columns(t, kc))
            mm.then_inc(S("dt_mm"), 1)

            def front(g, j):
                T = T_SSM + 6 * g + j
                wblocks(T, G_SSM + 6 * g + j, j % 2, j % 2, hT, range(KC), 0, KC, chunk)\
                    .then_inc(S("tile_done"), 1)

            def blk(t, c):
                return t[:, c * P:(c + 1) * P]

            def cb_and_turns(g):
                pe.wait_ge(S("bc_lo"), 2 * g + 3)
                pe.wait_ge(S("cb_masked"), g + 1)
                for c in range(NQB):
                    mm = hilo(blk(CB, c), bc[0], bc[1], True, True, lambda t: blk(t, c), lambda t: blk(t, c))
                mm.then_inc(S("cb"), 1)
                pe.wait_ge(S("y_sum"), 2 * g + 1)
                for b, src, n, name in ((TR, xs[0], 4, "x0_turned"), (YD, xs[1], 4, "x1_turned"),
                                        (YO, xs[2], 3, "b_turned")):
                    for c in range(n):
                        mm = pe.transpose(blk(b, c), blk(src, c), ident[:])
                    mm.then_inc(S(name), 1)

            def chunk_state(g, c):
                if c == 0:
                    pe.wait_ge(S("xd_lo"), g + 2)
                    pe.wait_ge(S("bt_lo"), g + 1)
                pe.wait_ge(S("state_out"), 3 * g + (3 if c == 2 else 1))
                hilo(STB[:, (c % 2) * 2 * P:(c % 2 + 1) * 2 * P], bt, xd, True, True,
                     lambda t: blk(t, c), lambda t: t[:, c, :]).then_inc(S("state_mm"), 1)

            def y_diag(g, t):
                if t == 0:
                    pe.wait_ge(S("xp_lo"), g + 1)
                else:
                    pe.wait_ge(S("y_sum"), 2 * g + 2)
                pe.wait_ge(S("m_lo"), HPG * g + 2 * t + 3)
                for c in range(NQB):
                    for r in range(2):
                        mm = hilo(blk(YD, c), xp[2 * t + r], mm_[r], r == 0, r == 1,
                                  lambda w: w[:, c, :], lambda w: blk(w, c))
                mm.then_inc(S("y_diag"), 1)

            def y_off(g, t):
                pe.wait_ge(S("prev_lo"), 3 * g + 3)
                for c in range(1, NQB):
                    mm = hilo(blk(YO, c), prev, bc[1], True, True,
                              lambda w: blk(w, 2 * (c - 1) + t), lambda w: blk(w, c))
                mm.then_inc(S("y_off"), 1)

            def group_ms(g):
                pe.wait_ge(S("g_sq"), 2 * g + 2)
                pe.wait_ge(S("g_ln"), g + 1)
                pe.matmul(NX[:], ones[:], sq[:], start=True, stop=False)
                pe.matmul(NX[:], ones[:], acc[:], start=False, stop=True).then_inc(S("g_ms"), 1)

            def ssm_section(back, ahead):
                def f(j):
                    if ahead is not None:
                        front(ahead, j)
                f(0)
                cb_and_turns(back)
                f(1)
                chunk_state(back, 0)
                chunk_state(back, 1)
                f(2)
                chunk_state(back, 2)
                y_diag(back, 0)
                f(3)
                y_off(back, 0)
                f(4)
                y_diag(back, 1)
                y_off(back, 1)
                f(5)
                group_ms(back)

            front(0, 0)
            front(0, 1)
            pe.wait_ge(S("acs"), 1)
            for c in range(NQB):
                pe.transpose(TR[:, c * SSM_HEADS:(c + 1) * SSM_HEADS], dt_t[4][:, c * P:(c + 1) * P],
                             ident[0:SSM_HEADS, 0:SSM_HEADS])
                mm = pe.transpose(TR[:, NH4 + c * SSM_HEADS:NH4 + (c + 1) * SSM_HEADS],
                                  dt_t[3][:, c * P:(c + 1) * P], ident[0:SSM_HEADS, 0:SSM_HEADS])
            mm.then_inc(S("acs_turned"), 1)
            front(0, 2)
            pe.wait_ge(S("acs_T"), 1)
            pe.matmul(YD[:, 0:NH4], last_row[:], acsT[:], start=True, stop=True).then_inc(S("acs_end"), 1)
            for j in range(3, 6):
                front(0, j)
            with pe.Fori(0, GROUPS - 1) as g:
                ssm_section(g, g + 1)
            ssm_section(GROUPS - 1, None)

            for half in range(2):
                for kc in range(KC):
                    pe.wait_ge(S("gs_lo"), half * KC + kc + 1)
                    mm = wblocks(T_SO + half, G_SO, half, 0, gs, [kc], half * KC, 2 * KC, chunk)
                mm.then_inc(S("tile_done"), 1)

            def so(i, js):
                for j in js:
                    m, half = j // 2, j % 2
                    wblocks(T_SO + 4 * i + j, G_SO + 2 * i + m, half, m, gs, range(KC), half * KC, 2 * KC, chunk)\
                        .then_inc(S("tile_done"), 1)
            so(0, (2, 3))
            with pe.Fori(1, KC // 2) as i:
                so(i, range(4))
            sum_squares(3)

            ffn(1, 4)

        @block.scalar
        def _(act_e):
            def w_hi_part(T, half, r):
                act_e.wait_ge(S(f"w_in{r}"), 16 * (half + 1))
                act_e.wait_ge(S("tile_done"), T + 1)
                act_e.activation(w_hi[r][:], raw[r][:], ACT.Copy).then_inc(S("w_hi"), 1)

            def inv_rms(n):
                act_e.wait_ge(S("ms"), n + 1)
                act_e.activation(sq[:], XB[:], ACT.Ln, bias=eps_c[:, 0:1], scale=1.0 / DM).then_inc(S("ln"), 1)
                act_e.wait_ge(S("ln"), n + 1)
                act_e.activation(rb[:], sq[:], ACT.Exp, scale=-0.5).then_inc(S("rb"), 1)

            def apart():
                act_e.sem_inc(S("act_waited"), 1)

            def x_chunk(R, c, n, keep=True):
                apart()
                if keep:
                    act_e.activation(columns(hT[0], c), columns(x, c), ACT.Copy,
                                     scale=columns(gain, n * KC + c, 1)).then_inc(S("h_hi"), 1)
                act_e.wait_ge(S("sq_sum"), R + 1)
                apart()
                act_e.activation(sq[:], columns(x, c), ACT.Square).then_inc(S("sq"), 1)

            act_e.nop().then_inc(S("exp"), 2)
            act_e.nop().then_inc(S("d_ln"), 1)
            act_e.wait_ge(S("small_in"), 16 * 8)
            act_e.wait_ge(S("ff_in"), 16)
            act_e.activation(ff_w[1][:], ff_w[0][:], ACT.Copy).then_inc(S("ff_w_hi"), 1)
            w_hi_part(0, 0, 0)
            for c in range(KC):
                act_e.wait_ge(S(f"x_in{c}"), 16)
                x_chunk(c, c, 0)
            act_e.wait_ge(S("setup"), 5)
            inv_rms(0)
            act_e.wait_ge(S("lam"), 2)
            act_e.activation(lams[:, 2:4], lams[:, 0:2], ACT.Exp).then_inc(S("lam_exp"), 1)
            act_e.wait_ge(S("ff_abs"), 1)
            act_e.activation(ff_t[2][:], ff_t[1][:], ACT.Exp, scale=-1.0).then_inc(S("ff_exp"), 1)
            act_e.wait_ge(S("ff_rows"), 2)
            for part in range(2):
                act_e.dma_start(rows_dram[part * FOX_HEADS:(part + 1) * FOX_HEADS, :],
                                ff_c[part][:].bitcast(F32)).then_inc(S("rows_stored"), 16)
            act_e.wait_ge(S("rows_stored"), 32)
            act_e.dma_start(crow[:].bitcast(F32), rows_dram.rearrange("(o h) n -> o (h n)", o=2))\
                .then_inc(S("crow_in"), 16)

            def exps(n, s):
                N = (s + 1) * P
                for m in range(2):
                    act_e.wait_ge(S("max"), 8 * n + 2 * s + m + 1)
                    act_e.wait_ge(S("turned"), 4 * n + s + 1)
                    act_e.activation(pr[s % 2][m][:, 0:N], SB[m][:, 0:N], ACT.Exp, bias=negmax[:, s % 2, m:m + 1],
                                     accum_out=rowsum[:, s % 2, m:m + 1]).then_inc(S("exp"), 1)

            def p_hi(k, n, s):
                N = (s + 1) * P
                act_e.wait_ge(S("turned"), 4 * n + s + 3)
                for m in range(2 if k == "f" else 1):
                    last = act_e.activation(pt[m][0][:, 0:N], TB[m][:, 0:N], ACT.Copy)
                last.then_inc(S("pT_hi"), 1)

            def v_hi(k, n):
                act_e.wait_ge(S("v_turned"), n + 2)
                act_e.wait_ge(S("pv"), 4 * n + 1)
                turned = XB[:].rearrange("p (b d) -> p b d", d=P)
                if k == "f":
                    for m in range(2):
                        half = slice(HD * m, HD * (m + 1))
                        last = act_e.activation(vs[k][m][0][:, :, half], turned[:, :, half], ACT.Copy)
                else:
                    last = act_e.activation(vs[k][0][0][:], turned, ACT.Copy)
                last.then_inc(S("v_hi"), 1)

            def swap(u, r, T):
                act_e.wait_ge(S("g_out"), T + 3)
                act_e.wait_ge(S("rope_b"), 2 * u + r + 1)
                for m in range(4):
                    to, of = 32 * (m ^ 1), 32 * m
                    last = act_e.activation(sw[to:to + 32, :], ev[r][of:of + 32, :], ACT.Copy)
                last.then_inc(S("swapped"), 1)

            def qk_hi(k, u, n, r, T):
                if k == "d":
                    act_e.wait_ge(S("rope"), 2 * u + r + 2)
                else:
                    act_e.wait_ge(S("g_out"), T + 3)
                act_e.wait_ge(S("s"), 8 * n + 1)
                act_e.activation((qs, ks)[r][k][0][:], ev[r][:], ACT.Copy).then_inc(S("qk"[r] + "_hi"), 1)

            def out_hi(k, u, n):
                act_e.wait_ge(S("pv"), 4 * n + 9)
                if k == "f":
                    apart()
                    act_e.activation(columns(yT[0], u), OB[:], ACT.Copy).then_inc(S("y_hi"), 1)
                    return
                act_e.activation(dsq[:], OB[:], ACT.Square).then_inc(S("d_sq"), 1)
                act_e.wait_ge(S("d_ms"), u + 1)
                act_e.wait_ge(S("o_out"), n)
                act_e.activation(drs[:], XB[:], ACT.Ln, bias=eps_c[:, 0:1], scale=1.0 / P).then_inc(S("d_ln"), 1)
                act_e.wait_ge(S("d_ln"), u + 2)
                act_e.activation(drs[:], drs[:], ACT.Exp, scale=-0.5).then_inc(S("d_rs"), 1)
                act_e.wait_ge(S("o_out"), n + 2)
                apart()
                act_e.activation(columns(yT[0], u + UNITS), dy[:], ACT.Copy).then_inc(S("y_hi"), 1)

            def section(att, proj):
                if proj:
                    kp, up = proj
                    np_, j0 = 2 * up + (kp == "d"), 3 * (kp == "d")
                    T0 = T_ATTN + 6 * up + j0

                def w(j):
                    if proj:
                        jj = j0 + j
                        w_hi_part(T0 + j, T_ATTN // 2 + 3 * up + jj // 2, jj % 2)

                def qk(r):
                    if proj:
                        qk_hi(kp, up, np_, r, T0 + 1 + r)

                def qk_swap(r):
                    if proj and kp == "d":
                        swap(up, r, T0 + 1 + r)
                if att is None:
                    for j in (1, 2, 3):
                        w(j)
                    v_hi(kp, np_)
                    qk(0)
                    qk(1)
                    return
                k, u = att
                n = 2 * u + (k == "d")
                w(1)
                exps(n, 0)
                w(2)
                exps(n, 1)
                p_hi(k, n, 0)
                if proj:
                    v_hi(kp, np_)
                exps(n, 2)
                p_hi(k, n, 1)
                w(3)
                qk_swap(0)
                exps(n, 3)
                qk(0)
                p_hi(k, n, 2)
                p_hi(k, n, 3)
                qk_swap(1)
                qk(1)
                out_hi(k, u, n)

            section(None, ("f", 0))
            with act_e.Fori(0, UNITS - 1) as i:
                section(("f", i), ("d", i))
                section(("d", i), ("f", i + 1))
            section(("f", UNITS - 1), ("d", UNITS - 1))
            section(("d", UNITS - 1), None)

            def residual(T, R, c, n, keep=True):
                act_e.wait_ge(S("x_add"), R - KC + 1)
                x_chunk(R, c, n, keep)

            with act_e.Fori(0, KC // 2) as i:
                for j in range(2):
                    w_hi_part(T_AO + 2 * i + j + 1, T_AO // 2 + i + (j + 1) // 2, (j + 1) % 2)
                    if j == 0:
                        act_e.wait_ge(S("rb"), 1)
                    residual(T_AO + 2 * i + j, RES_AO + 2 * i + j, 2 * i + j, 1)
            inv_rms(1)

            def ffn(l, R, norm):
                with act_e.Fori(0, FC) as i:
                    w_hi_part(T_GU[l] + 2 * i + 1, T_GU[l] // 2 + i, 1)
                    act_e.wait_ge(S("ffn_z"), FC * l + i + 1)
                    act_e.activation(ft[:], fz[:], ACT.Tanh).then_inc(S("ffn_tanh"), 1)
                    w_hi_part(T_GU[l] + 2 * i + 2, T_GU[l] // 2 + i + 1, 0)
                    act_e.wait_ge(S("ffn_act"), FC * l + i + 1)
                    apart()
                    act_e.activation(columns(act[0], i), fa[:], ACT.Copy).then_inc(S("act_hi"), 1)
                last = l == 1
                if l == 0:
                    act_e.wait_ge(S("dt_in"), 16)
                    copy_ = act_e.activation(dt_w[1][:], dt_w[0][:], ACT.Copy)
                    copy_.then_inc(S("dt_w_hi"), 1)

                def down(i, final):
                    for j in range(6):
                        T = T_DN[l] + 6 * i + j
                        if not (final and j == 5):
                            w_hi_part(T + 1, T_DN[l] // 2 + 3 * i + (j + 1) // 2, (j + 1) % 2)
                        if j == 0:
                            act_e.wait_ge(S("rb"), norm)
                        if j % 3 == 2:
                            residual(T, R + 2 * i + j // 3, 2 * i + j // 3, norm, not last)
                with act_e.Fori(0, KC // 2 - last) as i:
                    down(i, False)
                if last:
                    down(KC // 2 - 1, True)
                inv_rms(norm)

            ffn(0, RES_DN0, 2)

            CB, TR, STB, YD, YO, NX = SB[0], SB[1], TB[0], TB[1], OB, XB

            def copy(out, in_):
                return act_e.activation(out, in_, ACT.Copy)

            def tanh(n, src, buf, ready, value):
                act_e.wait_ge(S(ready), value)
                act_e.wait_ge(S("silu"), n + 1)
                act_e.activation(tt[buf][:], src[:], ACT.Tanh).then_inc(S("tanh"), 1)

            def w(g, j):
                w_hi_part(T_SSM + 6 * g + j + 1, T_SSM // 2 + 3 * g + (j + 1) // 2, (j + 1) % 2)

            def conv_tanh(g, j):
                tanh(6 * g + j, xs[j], j % 2, "conv", 16 * g + 4 * j + 5)

            def bc_hi(g, j):
                act_e.wait_ge(S("silu"), 6 * g + j + 5)
                if j == 1:
                    act_e.wait_ge(S("y_off"), 2 * g + 2)
                copy(bc[j][0][:], xs[2 + j][:]).then_inc(S("bc_hi"), 1)

            act_e.nop().then_inc(S("g_ln"), 1)
            act_e.activation(acol[:], hp[:, 1:2], ACT.Exp).then_inc(S("A_exp"), 1)
            w(0, 0)
            act_e.wait_ge(S("dt_abs"), 1)
            act_e.activation(dt_t[2][:], dt_t[1][:], ACT.Exp, scale=-1.0).then_inc(S("dt_exp"), 1)
            w(0, 1)
            w(0, 2)
            act_e.wait_ge(S("acs"), 1)
            act_e.dma_start(acs_dram, dt_t[4][:]).then_inc(S("acs_stored"), 16)
            act_e.wait_ge(S("dec_T"), 1)
            act_e.activation(dsT[:], decT[:], ACT.Exp).then_inc(S("decays"), 1)
            act_e.activation(cdT[:], YD[:, 0:NH4], ACT.Exp).then_inc(S("decays"), 1)
            for j in range(3, 6):
                w(0, j)
            for j in range(4):
                conv_tanh(0, j)
            for j in range(2):
                bc_hi(0, j)

            def exp_rows(g):
                act_e.wait_ge(S("ab_in"), 16 * (g + 1))
                act_e.wait_ge(S("y_sum"), 2 * g + 1)
                for t in range(2):
                    for h in range(2):
                        half = slice(HD * h, HD * (h + 1))
                        last = act_e.activation(ea[t][half, :], ab[half, (2 * t + h) * SEQ:(2 * t + h + 1) * SEQ],
                                                ACT.Exp)
                last.then_inc(S("ea"), 1)

            def decay_exp(g, r):
                act_e.wait_ge(S("decay_arg"), HPG * g + r + 1)
                act_e.activation(ab[:, r * SEQ:(r + 1) * SEQ], ab[:, r * SEQ:(r + 1) * SEQ], ACT.Exp)\
                    .then_inc(S("decay"), 1)

            def xp_hi(g):
                act_e.wait_ge(S("x_dt"), g + 1)
                act_e.wait_ge(S("y_diag"), 2 * g + 1)
                for r in range(HPG):
                    half = slice(HD * (r % 2), HD * (r % 2 + 1))
                    last = copy(xp[r][0][:, :, half], xst[:, :, HD * r:HD * (r + 1)])
                last.then_inc(S("xp_hi"), 1)

            def m_hi(g, r):
                act_e.wait_ge(S("m"), HPG * g + r + 2)
                act_e.wait_ge(S("y_diag"), 2 * g + r // 2 + 1)
                copy(mm_[r % 2][0][:], ab[:, r * SEQ:(r + 1) * SEQ]).then_inc(S("m_hi"), 1)

            def prev_hi(g, c):
                act_e.wait_ge(S("state_out"), 3 * g + c + 2)
                if c == 0:
                    act_e.wait_ge(S("y_off"), 2 * g + 2)
                copy(prev[0][:, c * 2 * P:(c + 1) * 2 * P], state[c % 2][:]).then_inc(S("prev_hi"), 1)

            def g_square(g, t):
                act_e.wait_ge(S("gated"), 2 * g + t + 3)
                act_e.wait_ge(S("g_ms"), g + 1)
                apart()
                act_e.activation((sq, acc)[t][:], columns(gT, 2 * g + t), ACT.Square).then_inc(S("g_sq"), 1)

            def ssm_section(g, ahead):
                def wf(j):
                    if ahead is not None:
                        w(ahead, j)

                def tf(j):
                    if ahead is not None:
                        conv_tanh(ahead, j)
                wf(0)
                for t in range(2):
                    tanh(6 * g + 4 + t, zc[t], t, "g_out", G_SSM + 6 * g + 4 + t + 3)
                exp_rows(g)
                for r in range(2):
                    decay_exp(g, r)
                wf(1)
                act_e.wait_ge(S("b_turned"), g + 2)
                act_e.wait_ge(S("state_mm"), 3 * g + 1)
                copy(bt[0][:], YO[:, 0:3 * P]).then_inc(S("bt_hi"), 1)
                xp_hi(g)
                for r in range(2, 4):
                    decay_exp(g, r)
                m_hi(g, 0)
                m_hi(g, 1)
                act_e.wait_ge(S("x_decayed"), g + 1)
                copy(xd[0][:], xst[:, 0:3, :]).then_inc(S("xd_hi"), 1)
                wf(2)
                tf(0)
                prev_hi(g, 0)
                prev_hi(g, 1)
                prev_hi(g, 2)
                m_hi(g, 2)
                wf(3)
                m_hi(g, 3)
                tf(1)
                g_square(g, 0)
                wf(4)
                tf(2)
                g_square(g, 1)
                wf(5)
                tf(3)
                if ahead is not None:
                    bc_hi(ahead, 0)
                    bc_hi(ahead, 1)
                act_e.wait_ge(S("g_ms"), g + 2)
                act_e.wait_ge(S("g_norm"), 2 * g + 1)
                act_e.activation(rg[:], NX[:], ACT.Ln, bias=eps_c[:, 1:2], scale=1.0 / (2 * P)).then_inc(S("g_ln"), 1)
                act_e.wait_ge(S("g_ln"), g + 2)
                act_e.activation(rg[:], rg[:], ACT.Exp, scale=-0.5).then_inc(S("rg"), 1)

            with act_e.Fori(0, GROUPS - 1) as g:
                ssm_section(g, g + 1)
            ssm_section(GROUPS - 1, None)

            with act_e.Fori(0, 2 * GROUPS) as c:
                act_e.wait_ge(S("g_norm"), 2 * GROUPS + 1)
                apart()
                act_e.activation(columns(gs[0], c), columns(gT, c), ACT.Copy).then_inc(S("gs_hi"), 1)
            with act_e.Fori(0, KC // 2) as i:
                for j in range(4):
                    T = T_SO + 4 * i + j
                    w_hi_part(T + 1, T_SO // 2 + 2 * i + (j + 1) // 2, (j + 1) % 2)
                    if j == 0:
                        act_e.wait_ge(S("setup"), 8)
                    if j % 2 == 1:
                        residual(T, RES_SO + 2 * i + j // 2, 2 * i + j // 2, 3)
            inv_rms(3)

            ffn(1, RES_DN1, 4)

        @block.vector
        def _(dve):
            made = [0]

            def link(ins):
                made[0] += 1
                ins.then_inc(S("dve_step"), 1)
                dve.wait_ge(S("dve_step"), made[0])

            def x_chunk(R, c, n, keep=True):
                if keep:
                    dve.wait_ge(S("h_hi"), R + 1)
                    dve.scalar_tensor_tensor(out=columns(hT[1], c), in0=columns(x, c),
                                             scalar=columns(gain, n * KC + c, 1),
                                             in1=columns(hT[0], c).bitcast(F32), op0=ALU.mult,
                                             op1=ALU.subtract).then_inc(S("h_lo"), 1)
                dve.wait_ge(S("sq"), R + 1)
                dve.wait_ge(S("sq_sum"), R + 1)
                dve.tensor_tensor(acc[:], acc[:], sq[:], ALU.add).then_inc(S("sq_sum"), 1)

            for name, credit in (("g_out", 2), ("v_lo", 1), ("q_lo", 1), ("k_lo", 1), ("rope_b", 1), ("rope", 1),
                                 ("o_out", 1), ("dy_lo", 1), ("sq_sum", 1)):
                dve.nop().then_inc(S(name), credit)
            dve.memset(eps_c[:, 0:1], EPS).then_inc(S("setup"), 1)
            dve.memset(eps_c[:, 1:2], GATED_EPS).then_inc(S("setup"), 1)
            dve.memset(acc[:], 0.0).then_inc(S("setup"), 1)
            dve.wait_ge(S("consts"), 8)
            dve.tensor_copy(ident_r[:], ident[:]).then_inc(S("setup"), 1)
            dve.tensor_copy(negmask_r[:], negmask[:]).then_inc(S("setup"), 1)
            dve.tensor_copy(ones2[:], ones[0:2, :]).then_inc(S("setup"), 1)
            dve.wait_ge(S("small_in"), 16 * 8)
            dve.wait_ge(S("setup"), 6)
            for c in range(KC):
                x_chunk(c, c, 0)
            for h in range(2):
                link(dve.tensor_tensor(lamp[:, h, :], lamt[:, 2 * h, :], lamt[:, 2 * h + 1, :], ALU.mult))
            for h in range(2):
                dve.tensor_reduce(lams[:, h:h + 1], lamp[:, h, :], AX.X, ALU.add).then_inc(S("lam"), 1)
            link(dve.tensor_scalar(sublnw[:], sublnw[:], 1.0 - LAM_INIT, None, ALU.mult))
            dve.wait_ge(S("lam_exp"), 1)
            link(dve.tensor_tensor(lams[:, 0:1], lams[:, 3:4], lams[:, 2:3], ALU.subtract))
            link(dve.tensor_scalar(neglam[:], lams[:, 0:1], -LAM_INIT, None, ALU.add))

            def softplus(t, exp_done, abs_done):
                dve.scalar_tensor_tensor(out=t[1][:], in0=t[0][:], scalar=-1.0, in1=t[0][:], op0=ALU.mult,
                                         op1=ALU.max).then_inc(S(abs_done), 1)
                dve.wait_ge(S(exp_done), 1)
                e = t[2]
                link(dve.tensor_scalar(t[1][:], e[:], 2.0, None, ALU.add))
                link(dve.reciprocal(t[3][:], t[1][:]))
                link(dve.tensor_tensor(t[4][:], e[:], t[3][:], ALU.mult))
                link(dve.tensor_tensor(t[1][:], t[4][:], t[4][:], ALU.mult))
                link(dve.tensor_scalar(t[3][:], t[1][:], 1.0 / (2 * LOG1P_TERMS + 1), None, ALU.mult))
                for n in range(LOG1P_TERMS - 1, 0, -1):
                    link(dve.scalar_tensor_tensor(out=t[3][:], in0=t[3][:], scalar=1.0 / (2 * n + 1), in1=t[1][:],
                                                  op0=ALU.add, op1=ALU.mult))
                link(dve.scalar_tensor_tensor(out=t[3][:], in0=t[3][:], scalar=1.0, in1=t[4][:],
                                              op0=ALU.add, op1=ALU.mult))
                link(dve.tensor_scalar(t[1][:], t[0][:], 0.0, None, ALU.max))
                link(dve.scalar_tensor_tensor(out=t[3][:], in0=t[3][:], scalar=2.0, in1=t[1][:],
                                              op0=ALU.mult, op1=ALU.add))

            dve.wait_ge(S("rb"), 1)
            dve.wait_ge(S("ff_mm"), 1)
            link(dve.tensor_tensor(ff_t[1][:], OB[0:FOX_HEADS, :], rb[0:FOX_HEADS, :], ALU.mult))
            link(dve.tensor_scalar(ff_t[0][:], ff_t[1][:], bff[:, 0:1], -1.0, ALU.add, ALU.mult))
            softplus(ff_t, "ff_exp", "ff_abs")
            link(dve.memset(ff_t[1][:], 1.0))
            link(dve.tensor_tensor_scan(ff_t[4][:], ff_t[1][:], ff_t[3][:], 0.0, ALU.mult, ALU.add))
            dve.tensor_copy(ff_c[0][:], ff_t[4][:]).then_inc(S("ff_rows"), 1)
            dve.wait_ge(S("ff_rows"), 1)
            dve.tensor_tensor(ff_c[1][:], ff_t[4][:], ff_c[0][:].bitcast(F32), ALU.subtract).then_inc(S("ff_rows"), 1)

            def scores_max(n, s):
                for m in range(2):
                    dve.wait_ge(S("s"), 8 * n + 2 * s + m + 10)
                    dve.tensor_reduce(negmax[:, s % 2, m:m + 1], SB[m][:, 0:(s + 1) * P], AX.X, ALU.max,
                                      negate=True).then_inc(S("max"), 1)

            def normalise(k, u, s):
                n, N = 2 * u + (k == "d"), (s + 1) * P
                p0, p1 = (pr[s % 2][m][:, 0:N] for m in range(2))
                r0, r1 = (rinv[:, s % 2, m:m + 1] for m in range(2))
                dve.wait_ge(S("exp"), 8 * n + 2 * s + 4)
                dve.reciprocal(rinv[:, s % 2, :], rowsum[:, s % 2, :]).then_inc(S("rinv"), 1)
                dve.wait_ge(S("rinv"), 4 * n + s + 1)
                if k == "f":
                    dve.tensor_scalar(p0, p0, r0, None, ALU.mult)
                    dve.tensor_scalar(p1, p1, r1, None, ALU.mult).then_inc(S("p"), 1)
                else:
                    dve.tensor_scalar(p1, p1, r1, neglam[:, 0:1], ALU.mult, ALU.mult).then_inc(S("p1"), 1)
                    dve.wait_ge(S("p1"), 4 * u + s + 1)
                    dve.scalar_tensor_tensor(out=p0, in0=p0, scalar=r0, in1=p1, op0=ALU.mult,
                                             op1=ALU.add).then_inc(S("p"), 1)

            def p_lo(k, n, s):
                N = (s + 1) * P
                dve.wait_ge(S("pT_hi"), 4 * n + s + 1)
                for m in range(2 if k == "f" else 1):
                    last = dve.tensor_tensor(pt[m][1][:, 0:N], TB[m][:, 0:N], pt[m][0][:, 0:N].bitcast(F32),
                                             ALU.subtract)
                last.then_inc(S("pT_lo"), 1)

            def v_out(n, T, bank_):
                dve.wait_ge(S("tile_done"), T + 3)
                dve.wait_ge(S("v_turned"), n + 1)
                dve.tensor_tensor(vt[:], bank_[:], rb[:], ALU.mult).then_inc(S("g_out"), 1)

            def v_lo_part(k, n):
                dve.wait_ge(S("v_hi"), n + 1)
                turned = XB[:].rearrange("p (b d) -> p b d", d=P)
                if k == "f":
                    for m in range(2):
                        half = slice(HD * m, HD * (m + 1))
                        last = dve.tensor_tensor(vs[k][m][1][:, :, half], turned[:, :, half],
                                                 vs[k][m][0][:, :, half].bitcast(F32), ALU.subtract)
                else:
                    last = dve.tensor_tensor(vs[k][0][1][:], turned, vs[k][0][0][:].bitcast(F32), ALU.subtract)
                last.then_inc(S("v_lo"), 1)

            def qk_out(n, r, T, bank_):
                dve.wait_ge(S("tile_done"), T + 3)
                dve.wait_ge(S("qk"[r] + "_lo"), n + 1)
                dve.scalar_tensor_tensor(out=ev[r][:], in0=bank_[:], scalar=(HD ** -0.5, 1.0)[r], in1=rb[:],
                                         op0=ALU.mult, op1=ALU.mult).then_inc(S("g_out"), 1)

            def rope_cos(u, r, T):
                dve.wait_ge(S("g_out"), T + 3)
                dve.wait_ge(S("rope"), 2 * u + r + 1)
                dve.tensor_tensor(rot[:], ev[r][:], cos[:], ALU.mult).then_inc(S("rope_a"), 1)

            def rope_sin(u, r):
                dve.wait_ge(S("swapped"), 2 * u + r + 1)
                dve.tensor_tensor(sw[:], sw[:], sin[:], ALU.mult).then_inc(S("rope_b"), 1)
                dve.wait_ge(S("rope_a"), 2 * u + r + 1)
                dve.wait_ge(S("rope_b"), 2 * u + r + 2)
                dve.tensor_tensor(ev[r][:], rot[:], sw[:], ALU.add).then_inc(S("rope"), 1)

            def qk_lo_part(k, n, r):
                dve.wait_ge(S("qk"[r] + "_hi"), n + 1)
                t = (qs, ks)[r][k]
                dve.tensor_tensor(t[1][:], ev[r][:], t[0][:].bitcast(F32), ALU.subtract)\
                    .then_inc(S("qk"[r] + "_lo"), 1)

            def out_lo(k, u, n):
                if k == "f":
                    dve.wait_ge(S("y_hi"), n + 1)
                    dve.tensor_tensor(columns(yT[1], u), OB[:], columns(yT[0], u).bitcast(F32), ALU.subtract)\
                        .then_inc(S("o_out"), 1)
                    return
                dve.wait_ge(S("d_rs"), u + 1)
                dve.wait_ge(S("dy_lo"), u + 1)
                dve.scalar_tensor_tensor(out=dy[:], in0=OB[:], scalar=sublnw[:, 0:1], in1=drs[:], op0=ALU.mult,
                                         op1=ALU.mult).then_inc(S("o_out"), 1)
                dve.wait_ge(S("y_hi"), n + 1)
                dve.tensor_tensor(columns(yT[1], u + UNITS), dy[:], columns(yT[0], u + UNITS).bitcast(F32),
                                  ALU.subtract).then_inc(S("dy_lo"), 1)

            def section(att, proj):
                if proj:
                    kp, up = proj
                    np_, j0 = 2 * up + (kp == "d"), 3 * (kp == "d")
                    T0 = T_ATTN + 6 * up + j0

                def v_first():
                    if proj:
                        v_out(np_, T0, GB[j0 % 2])

                def qk_first(r):
                    if proj:
                        qk_out(np_, r, T0 + 1 + r, GB[(j0 + 1 + r) % 2])
                        if kp == "d":
                            rope_cos(up, r, T0 + 1 + r)

                def qk_turn(r):
                    if proj and kp == "d":
                        rope_sin(up, r)

                def qk_lo(r):
                    if proj:
                        qk_lo_part(kp, np_, r)
                if att is None:
                    v_first()
                    v_lo_part(kp, np_)
                    for r in range(2):
                        qk_first(r)
                    for r in range(2):
                        qk_lo(r)
                    return
                k, u = att
                n = 2 * u + (k == "d")
                scores_max(n, 0)
                normalise(k, u, 0)
                v_first()
                scores_max(n, 1)
                p_lo(k, n, 0)
                normalise(k, u, 1)
                scores_max(n, 2)
                if proj:
                    v_lo_part(kp, np_)
                p_lo(k, n, 1)
                qk_first(0)
                normalise(k, u, 2)
                scores_max(n, 3)
                qk_turn(0)
                p_lo(k, n, 2)
                qk_lo(0)
                normalise(k, u, 3)
                p_lo(k, n, 3)
                qk_first(1)
                qk_turn(1)
                qk_lo(1)
                out_lo(k, u, n)

            section(None, ("f", 0))
            with dve.Fori(0, UNITS - 1) as i:
                section(("f", i), ("d", i))
                section(("d", i), ("f", i + 1))
            section(("f", UNITS - 1), ("d", UNITS - 1))
            section(("d", UNITS - 1), None)

            def residual(T, R, c, n, bank_, keep=True):
                dve.wait_ge(S("tile_done"), T + 3)
                dve.tensor_tensor(columns(x, c), columns(x, c), bank_[:], ALU.add).then_inc(S("x_add"), 1)

            dve.wait_ge(S("ms"), 1)
            dve.memset(acc[:], 0.0).then_inc(S("setup"), 1)
            dve.wait_ge(S("setup"), 7)
            with dve.Fori(0, KC // 2) as i:
                for j in range(2):
                    residual(T_AO + 2 * i + j, RES_AO + 2 * i + j, 2 * i + j, 1, GB[j])
                    dve.wait_ge(S("x_add"), RES_AO - KC + 2 * i + j + 1)
                    dve.nop().then_inc(S("g_out"), 1)
                    x_chunk(RES_AO + 2 * i + j, 2 * i + j, 1)

            def ffn(l, R, norm, adds):
                with dve.Fori(0, FC) as i:
                    n, T = FC * l + i, T_GU[l] + 2 * i
                    dve.wait_ge(S("rb"), norm)
                    dve.wait_ge(S("tile_done"), T + 3)
                    dve.wait_ge(S("ffn_silu"), n + 1)
                    dve.scalar_tensor_tensor(out=fz[:], in0=GB[0][:], scalar=0.5, in1=rb[:], op0=ALU.mult,
                                             op1=ALU.mult).then_inc(S("ffn_z"), 1)
                    dve.wait_ge(S("ffn_z"), n + 1)
                    dve.nop().then_inc(S("g_out"), 1)
                    dve.wait_ge(S("ffn_tanh"), n + 1)
                    dve.scalar_tensor_tensor(out=fs[:], in0=ft[:], scalar=1.0, in1=fz[:], op0=ALU.add,
                                             op1=ALU.mult).then_inc(S("ffn_silu"), 1)
                    dve.wait_ge(S("tile_done"), T + 4)
                    dve.tensor_tensor(fu[:], GB[1][:], rb[:], ALU.mult).then_inc(S("g_out"), 1)
                    dve.wait_ge(S("ffn_silu"), n + 2)
                    dve.wait_ge(S("g_out"), G_GU[l] + 2 * i + 4)
                    dve.tensor_tensor(fa[:], fs[:], fu[:], ALU.mult).then_inc(S("ffn_act"), 1)
                    dve.wait_ge(S("act_hi"), n + 1)
                    dve.tensor_tensor(columns(act[1], i), fa[:], columns(act[0], i).bitcast(F32), ALU.subtract)\
                        .then_inc(S("act_lo"), 1)
                last = l == 1
                link(dve.memset(acc[:], 0.0))
                with dve.Fori(0, KC // 2) as i:
                    for m in range(2):
                        residual(T_DN[l] + 6 * i + 3 * m + 2, R + 2 * i + m, 2 * i + m, norm, GB[m])
                        dve.wait_ge(S("x_add"), R - KC + 2 * i + m + 1)
                        dve.nop().then_inc(S("g_out"), 1)
                        x_chunk(R + 2 * i + m, 2 * i + m, norm, not last)

            dve.nop().then_inc(S("ffn_silu"), 1)
            ffn(0, RES_DN0, 2, 0)

            CB, TR, STB, YD, YO, NX = SB[0], SB[1], TB[0], TB[1], OB, XB

            def u_out(g, j):
                dve.wait_ge(S("tile_done"), T_SSM + 6 * g + j + 3)
                if j < 4:
                    dve.wait_ge(S("conv"), 16 * g + 1)
                    dve.tensor_tensor(ub[j][:, 3:], GB[j % 2][:], rb[:], ALU.mult).then_inc(S("g_out"), 1)
                else:
                    dve.wait_ge(S("gated"), 2 * g + j - 3)
                    dve.scalar_tensor_tensor(out=zc[j - 4][:], in0=GB[j % 2][:], scalar=0.5, in1=rb[:],
                                             op0=ALU.mult, op1=ALU.mult).then_inc(S("g_out"), 1)

            def par(g, n):
                return columns(gp, g * GPW + n, 1)

            def conv(g, j):
                n = 16 * g + 4 * j
                dve.wait_ge(S("g_out"), G_SSM + 6 * g + j + 3)
                if j < 3:
                    dve.wait_ge(S("b_turned"), g + 1)
                else:
                    dve.wait_ge(S("bc_lo"), 2 * g + 1)
                dve.tensor_scalar(xs[j][:], ub[j][:, 3:], par(g, 5 * j + 3), par(g, 5 * j + 4), ALU.mult, ALU.add)\
                    .then_inc(S("conv"), 1)
                for k in range(3):
                    dve.wait_ge(S("conv"), n + k + 2)
                    dve.scalar_tensor_tensor(out=xs[j][:], in0=ub[j][:, k:k + SEQ], scalar=par(g, 5 * j + k),
                                             in1=xs[j][:], op0=ALU.mult, op1=ALU.add).then_inc(S("conv"), 1)

            def silu(n, t, par_):
                dve.wait_ge(S("tanh"), n + 1)
                dve.scalar_tensor_tensor(out=t[:], in0=tt[par_][:], scalar=1.0, in1=t[:], op0=ALU.add,
                                         op1=ALU.mult).then_inc(S("silu"), 1)

            def sub_lo(lo, src, hi, sem):
                return dve.tensor_tensor(lo, src, hi.bitcast(F32), ALU.subtract)

            def bc_lo(g, j):
                dve.wait_ge(S("bc_hi"), 2 * g + j + 1)
                dve.tensor_tensor(bc[j][1][:], xs[2 + j][:], bc[j][0][:].bitcast(F32), ALU.subtract)\
                    .then_inc(S("bc_lo"), 1)

            for name, credit in (("silu", 2), ("conv", 1), ("cb_masked", 1), ("y_sum", 1), ("state_out", 1),
                                 ("m_lo", 1), ("gated", 2), ("g_norm", 1), ("bc_lo", 1), ("m", 1)):
                dve.nop().then_inc(S(name), credit)
            link(dve.tensor_scalar(gp[:].rearrange("p (g n) -> p g n", n=GPW)[:, :, 0:20],
                                   gp[:].rearrange("p (g n) -> p g n", n=GPW)[:, :, 0:20], 0.5, None, ALU.mult))
            for j in range(4):
                dve.memset(ub[j][:, 0:3], 0.0)
            for r in range(HPG):
                for part in range(2):
                    last = dve.memset(xp[r][part][:, :, HD * (1 - r % 2):HD * (2 - r % 2)].bitcast(F32), 0.0)
            link(last)
            dve.wait_ge(S("rb"), 3)
            dve.wait_ge(S("dt_mm"), 1)
            link(dve.tensor_tensor(dt_t[1][:], CB[0:SSM_HEADS, :], rb[0:SSM_HEADS, :], ALU.mult))
            link(dve.tensor_scalar(dt_t[0][:], dt_t[1][:], hp[:, 0:1], None, ALU.add))
            u_out(0, 0)
            u_out(0, 1)
            softplus(dt_t, "dt_exp", "dt_abs")
            dve.wait_ge(S("A_exp"), 1)
            link(dve.tensor_scalar(dt_t[5][:], dt_t[3][:], acol[:, 0:1], -1.0, ALU.mult, ALU.mult))
            link(dve.memset(dt_t[1][:], 1.0))
            for c in range(NQB):
                cut = slice(c * P, (c + 1) * P)
                last = dve.tensor_tensor_scan(dt_t[4][:, cut], dt_t[1][:, cut], dt_t[5][:, cut], 0.0,
                                              ALU.mult, ALU.add)
            last.then_inc(S("acs"), 1)
            dve.wait_ge(S("acs_turned"), 1)
            dve.tensor_copy(acsT[:], TR[:, 0:NH4]).then_inc(S("acs_T"), 1)
            link(dve.tensor_copy(dtT[:], TR[:, NH4:2 * NH4]))
            link(dve.tensor_scalar(nacs[:], TR[:, 0:NH4], -1.0, None, ALU.mult))
            u_out(0, 2)
            dve.wait_ge(S("acs_end"), 1)
            dve.wait_ge(S("acs_T"), 1)
            dve.tensor_tensor(decT[:], YD[:, 0:NH4], acsT[:], ALU.subtract).then_inc(S("dec_T"), 1)
            for j in range(3, 6):
                u_out(0, j)
            for j in range(4):
                conv(0, j)
                silu(j, xs[j], j % 2)
            for j in range(2):
                bc_lo(0, j)
            dve.wait_ge(S("decays"), 2)

            def head_cols(t, g, t2, nchunks):
                at = HPG * g + 2 * t2
                v = t[:].rearrange("p (c h) -> p c h", h=SSM_HEADS)
                v = v[:, 0:nchunks, at:at + 2] if isinstance(at, int) else v[:, 0:nchunks, bass.ds(at, 2)]
                return v.unsqueeze(3).broadcast_to([P, nchunks, 2, HD])

            def decay_args(g, r):
                for c in range(NQB):
                    cut = ab[:, r * SEQ + c * P:r * SEQ + (c + 1) * P]
                    last = dve.tensor_scalar(cut, cut, width_at(nacs, c * SSM_HEADS + HPG * g + r, 1), 0.0,
                                             ALU.add, ALU.min)
                last.then_inc(S("decay_arg"), 1)

            def m_part(g, r):
                dve.wait_ge(S("decay"), HPG * g + r + 1)
                cut = ab[:, r * SEQ:(r + 1) * SEQ]
                dve.tensor_tensor(cut, cut, cbm[:], ALU.mult).then_inc(S("m"), 1)

            def m_lo(g, r):
                dve.wait_ge(S("m_hi"), HPG * g + r + 1)
                dve.tensor_tensor(mm_[r % 2][1][:], ab[:, r * SEQ:(r + 1) * SEQ], mm_[r % 2][0][:].bitcast(F32),
                                  ALU.subtract).then_inc(S("m_lo"), 1)

            def new_state(g, c):
                n = 3 * g + c
                dve.wait_ge(S("state_mm"), 3 * g + max(c, 1) + 2)
                dve.wait_ge(S("state_out"), n + 1)
                src = STB[:, (c % 2) * 2 * P:(c % 2 + 1) * 2 * P]
                if c == 0:
                    dve.tensor_copy(state[0][:], src).then_inc(S("state_out"), 1)
                    return
                if c == 2:
                    dve.wait_ge(S("prev_lo"), n - 1)
                for r in range(HPG):
                    cut = slice(HD * r, HD * (r + 1))
                    last = dve.scalar_tensor_tensor(
                        out=state[c % 2][:, cut], in0=state[(c + 1) % 2][:, cut],
                        scalar=width_at(cdT, c * SSM_HEADS + HPG * g + r, 1), in1=src[:, cut],
                        op0=ALU.mult, op1=ALU.add)
                last.then_inc(S("state_out"), 1)

            def prev_lo(g, c):
                dve.wait_ge(S("prev_hi"), 3 * g + c + 1)
                cut = slice(c * 2 * P, (c + 1) * 2 * P)
                dve.tensor_tensor(prev[1][:, cut], state[c % 2][:], prev[0][:, cut].bitcast(F32), ALU.subtract)\
                    .then_inc(S("prev_lo"), 1)

            def y_sum(g, t):
                y = columns(gT, 2 * g + t)
                y_late = width_at(gT, (2 * g + t) * SEQ + P, SEQ - P)
                dve.wait_ge(S("y_diag"), 2 * g + t + 2)
                dve.wait_ge(S("y_part"), 6 * g + 2)
                dve.tensor_tensor(y, y, YD[:], ALU.add).then_inc(S("y_part"), 1)
                dve.wait_ge(S("y_off"), 2 * g + t + 3)
                dve.wait_ge(S("ea"), g + 1)
                dve.tensor_tensor(ea[t][:, P:], YO[:, P:], ea[t][:, P:], ALU.mult).then_inc(S("y_part"), 1)
                dve.wait_ge(S("y_part"), 6 * g + 2 * t + 4)
                dve.tensor_tensor(y_late, y_late, ea[t][:, P:], ALU.add).then_inc(S("y_sum"), 1)

            def gate(g, t):
                dve.wait_ge(S("y_sum"), 2 * g + t + 2)
                dve.wait_ge(S("silu"), 6 * g + 8)
                y = columns(gT, 2 * g + t)
                dve.tensor_tensor(y, y, zc[t][:], ALU.mult).then_inc(S("gated"), 1)

            def ssm_section(g, ahead):
                def uf(j):
                    if ahead is not None:
                        u_out(ahead, j)

                def cf(j):
                    if ahead is not None:
                        conv(ahead, j)

                def sf(j):
                    if ahead is not None:
                        silu(6 * ahead + j, xs[j], j % 2)
                uf(0)
                dve.wait_ge(S("g_norm"), 2 * g + 1)
                for t in range(2):
                    dve.tensor_scalar(columns(gT, 2 * g + t), xs[t][:], par(g, 20 + t), None, ALU.mult).then_inc(S("y_part"), 1)
                for t in range(2):
                    silu(6 * g + 4 + t, zc[t], t)
                dve.wait_ge(S("ea"), g + 1)
                for r in range(HPG):
                    decay_args(g, r)
                dve.wait_ge(S("cb"), g + 1)
                dve.wait_ge(S("m"), HPG * g + 1)
                dve.tensor_tensor(cbm[:].rearrange("p (c l) -> p c l", l=P), CB[:].rearrange("p (c l) -> p c l", l=P),
                                  causal[:].unsqueeze(1).broadcast_to([P, NQB, P]), ALU.mult)\
                    .then_inc(S("cb_masked"), 1)
                dve.wait_ge(S("xd_lo"), g + 1)
                for t, b in enumerate((TR, YD)):
                    dve.wait_ge(S(f"x{t}_turned"), g + 1)
                    last = dve.tensor_tensor(
                        xst[:, :, t * P:(t + 1) * P].rearrange("p c (h d) -> p c h d", d=HD),
                        b[:].rearrange("p (c h d) -> p c h d", h=2, d=HD), head_cols(dtT, g, t, NQB), ALU.mult)
                last.then_inc(S("x_dt"), 1)
                dve.wait_ge(S("cb_masked"), g + 2)
                m_part(g, 0)
                m_part(g, 1)
                dve.wait_ge(S("bt_hi"), g + 1)
                dve.tensor_tensor(bt[1][:], YO[:, 0:3 * P], bt[0][:].bitcast(F32), ALU.subtract)\
                    .then_inc(S("bt_lo"), 1)
                dve.wait_ge(S("xp_hi"), g + 1)
                for r in range(HPG):
                    half = slice(HD * (r % 2), HD * (r % 2 + 1))
                    last = dve.tensor_tensor(xp[r][1][:, :, half], xst[:, :, HD * r:HD * (r + 1)],
                                             xp[r][0][:, :, half].bitcast(F32), ALU.subtract)
                last.then_inc(S("xp_lo"), 1)
                dve.wait_ge(S("xp_lo"), g + 1)
                for t in range(2):
                    cut = xst[:, 0:3, t * P:(t + 1) * P].rearrange("p c (h d) -> p c h d", d=HD)
                    last = dve.tensor_tensor(cut, cut, head_cols(dsT, g, t, 3), ALU.mult)
                last.then_inc(S("x_decayed"), 1)
                uf(1)
                m_lo(g, 0)
                m_lo(g, 1)
                dve.wait_ge(S("xd_hi"), g + 1)
                dve.tensor_tensor(xd[1][:], xst[:, 0:3, :], xd[0][:].bitcast(F32), ALU.subtract)\
                    .then_inc(S("xd_lo"), 1)
                cf(0)
                m_part(g, 2)
                m_part(g, 3)
                uf(2)
                new_state(g, 0)
                new_state(g, 1)
                sf(0)
                prev_lo(g, 0)
                new_state(g, 2)
                cf(1)
                prev_lo(g, 1)
                prev_lo(g, 2)
                uf(3)
                m_lo(g, 2)
                m_lo(g, 3)
                y_sum(g, 0)
                gate(g, 0)
                sf(1)
                cf(2)
                uf(4)
                y_sum(g, 1)
                gate(g, 1)
                sf(2)
                uf(5)
                cf(3)
                sf(3)
                if ahead is not None:
                    bc_lo(ahead, 0)
                    bc_lo(ahead, 1)
                dve.wait_ge(S("rg"), g + 1)
                for t in range(2):
                    dve.scalar_tensor_tensor(out=columns(gT, 2 * g + t), in0=columns(gT, 2 * g + t), scalar=par(g, 22 + t),
                                             in1=rg[:], op0=ALU.mult, op1=ALU.mult).then_inc(S("g_norm"), 1)

            dve.nop().then_inc(S("xd_lo"), 1)
            with dve.Fori(0, GROUPS - 1) as g:
                ssm_section(g, g + 1)
            ssm_section(GROUPS - 1, None)

            dve.wait_ge(S("g_norm"), 2 * GROUPS + 1)
            with dve.Fori(0, 2 * GROUPS) as c:
                dve.wait_ge(S("gs_hi"), c + 1)
                dve.tensor_tensor(columns(gs[1], c), columns(gT, c), columns(gs[0], c).bitcast(F32), ALU.subtract)\
                    .then_inc(S("gs_lo"), 1)
            dve.wait_ge(S("g_ms"), GROUPS + 1)
            dve.memset(acc[:], 0.0).then_inc(S("setup"), 1)
            dve.wait_ge(S("setup"), 8)
            with dve.Fori(0, KC // 2) as i:
                for m in range(2):
                    residual(T_SO + 4 * i + 2 * m + 1, RES_SO + 2 * i + m, 2 * i + m, 3, GB[m])
                    dve.wait_ge(S("x_add"), RES_SO - KC + 2 * i + m + 1)
                    dve.nop().then_inc(S("g_out"), 1)
                    x_chunk(RES_SO + 2 * i + m, 2 * i + m, 3)

            ffn(1, RES_DN1, 4, 0)

            dve.wait_ge(S("rb"), 5)
            for c in range(KC):
                dve.scalar_tensor_tensor(out=columns(x, c), in0=columns(x, c), scalar=columns(gain, 4 * KC + c, 1),
                                         in1=rb[:], op0=ALU.mult, op1=ALU.mult).then_inc(S("y_out"), 1)


def kernel(**inputs):
    import concourse.bacc as bacc
    from concourse.bass_utils import run_bass_kernel_spmd

    a = {k: np.asarray(v) for k, v in inputs.items()}

    def tiles(w, starts, pad=P):
        K = w.shape[0]
        return [w[:, c:c + P].reshape(K // P, P, P).transpose(1, 0, 2).reshape(P, K) for c in starts]

    wi = a["attn_w_in"][0]
    FW = FOX_HEADS * HD
    off = {"fq": 0, "fk": FW, "fv": 2 * FW, "ff": 3 * FW, "dq": 3 * FW + FOX_HEADS}
    off["dk"] = off["dq"] + FW
    off["dv"] = off["dk"] + FW
    arrays = {}
    arrays["xT"] = a["x"][0].T.reshape(KC, P, SEQ)
    ffw = np.zeros((DM, P), np.float32)
    ffw[:, 0:FOX_HEADS] = wi[:, off["ff"]:off["ff"] + FOX_HEADS]
    arrays["w_ff"] = tiles(ffw, [0])[0]
    arrays["w_attn"] = np.concatenate(tiles(wi, [off[k + r] + P * u for u in range(UNITS) for k in "fd" for r in "vqk"]))
    arrays["w_ao"] = np.concatenate(tiles(a["attn_w_out"][0], range(0, DM, P)))
    gu = [np.concatenate([t for g, u in zip(tiles(a["ffn_w_gate"][l], range(0, DFF, P)),
                                            tiles(a["ffn_w_up"][l], range(0, DFF, P))) for t in (g, u)])
          for l in range(2)]
    arrays["w_gu"] = np.stack(gu)
    arrays["w_dn"] = np.stack([np.concatenate(tiles(a["ffn_w_down"][l], range(0, DM, P))) for l in range(2)])
    wdt = np.zeros((DM, P), np.float32)
    SP_ = a["ssm_w_in"][0]
    conv_dim = DI + 2 * GROUPS * P
    wdt[:, 0:SSM_HEADS] = SP_[:, DI + conv_dim:]
    arrays["w_dt"] = tiles(wdt, [0])[0]
    xoff, boff, coff = DI, 2 * DI, 2 * DI + GROUPS * P
    arrays["w_ssm"] = np.concatenate(tiles(SP_, [o for g in range(GROUPS) for o in (
        xoff + 2 * P * g, xoff + 2 * P * g + P, boff + P * g, coff + P * g, 2 * P * g, 2 * P * g + P)]))
    arrays["w_so"] = np.concatenate(tiles(a["ssm_w_out"][0], range(0, DM, P)))
    arrays["ssm_heads"] = np.stack([a["ssm_dt_bias"][0], a["ssm_a_log"][0]], 1)
    taps = np.concatenate([a["ssm_conv_w"][0], a["ssm_conv_b"]]).reshape(5, 4 * GROUPS, P)
    d = np.repeat(a["ssm_d"][0], HD).reshape(2 * GROUPS, P)
    nw = a["ssm_norm"][0].reshape(2 * GROUPS, P)
    rows = []
    for g in range(GROUPS):
        for t in (2 * g, 2 * g + 1, 2 * GROUPS + g, 3 * GROUPS + g):
            rows += [taps[n, t] for n in range(5)]
        rows += [d[2 * g], d[2 * g + 1], nw[2 * g], nw[2 * g + 1]]
    arrays["ssm_params"] = np.stack(rows, 1)
    norms = [a["norm_mix"][0], a["norm_ffn"][0], a["norm_mix"][1], a["norm_ffn"][1], a["final_norm"]]
    arrays["gains"] = np.stack([n.reshape(KC, P).T for n in norms], 1).reshape(P, 5 * KC)
    arrays["fox_cols"] = a["attn_b_forget"][0].reshape(FOX_HEADS, 1)
    inv = np.float32(10000.0) ** (-np.arange(0, HD, 2, dtype=np.float32) / np.float32(HD))
    ang = np.arange(SEQ, dtype=np.float32)[:, None] * inv[None, :].astype(np.float32)
    c, s = np.cos(ang).T.astype(np.float32), np.sin(ang).T.astype(np.float32)
    arrays["rope"] = np.stack([np.concatenate([c] * 4), np.concatenate([-s, s] * 2)])
    arrays["lam"] = a["diff_lambda"][0]
    arrays["subln"] = a["diff_subln"][0].reshape(P, 1)
    arrays = {k: np.ascontiguousarray(v) for k, v in arrays.items()}

    nc = bacc.Bacc("TRN2", target_bir_lowering=False, num_devices=1)
    aps = {k: nc.dram_tensor("in_" + k, v.shape, F32, kind="ExternalInput").ap() for k, v in arrays.items()}
    aps["outT"] = nc.dram_tensor("outT", (KC, P, SEQ), F32, kind="ExternalOutput").ap()
    trunk(nc, **aps)
    r = run_bass_kernel_spmd(nc, [{"in_" + k: v for k, v in arrays.items()}], core_ids=[0])
    return np.ascontiguousarray(r.results[0]["outT"].reshape(DM, SEQ).T).reshape(1, SEQ, DM)
```

```python
from contextlib import ExitStack
import math

import numpy as np

import concourse.bass as bass
from concourse import mybir

F32 = mybir.dt.float32
F32R = mybir.dt.float32r
ALU = mybir.AluOpType
ACT = mybir.ActivationFunctionType
AX = mybir.AxisListType

P = 128
SEQ = 512
DM = 1024
KC = DM // P
NQB = SEQ // P
HD = 64
FOX_HEADS = 8
UNITS = 4
DFF = 2816
FC = DFF // P
DI = 2048
GROUPS = 8
HPG = 4
SSM_HEADS = 32
DOWN_CUT = (8, 8, 6)
EPS = 1e-6
GATED_EPS = 1e-5
LAM_INIT = 0.8 - 0.6 * math.exp(-0.3 * 0)
NEG = -1e30
GPW = 4 * 5 + 4
LOG1P_TERMS = 7

T_ATTN, G_ATTN = 0, 0
T_AO, G_AO = T_ATTN + 6 * UNITS, G_ATTN + 6 * UNITS
T_GU = [T_AO + KC, None]
G_GU = [G_AO + KC, None]
T_DN = [T_GU[0] + 2 * FC, None]
G_DN = [G_GU[0] + 2 * FC, None]
T_SSM, G_SSM = T_DN[0] + 3 * KC, G_DN[0] + KC
T_SO, G_SO = T_SSM + 6 * GROUPS, G_SSM + 6 * GROUPS
T_GU[1], G_GU[1] = T_SO + 2 * KC, G_SO + KC
T_DN[1], G_DN[1] = T_GU[1] + 2 * FC, G_GU[1] + 2 * FC
T_ALL = T_DN[1] + 3 * KC
RES_AO, RES_DN0, RES_SO, RES_DN1 = KC, 2 * KC, 3 * KC, 4 * KC


def columns(t, c, width=SEQ):
    return t[:, c * width:(c + 1) * width] if isinstance(c, int) else t[:, bass.ds(c * width, width)]


def first_columns(t, n):
    return t[:].rearrange("p (k m) -> p k m", m=P)[:, :, 0:n]


def width_at(t, at, n):
    return t[:, at:at + n] if isinstance(at, int) else t[:, bass.ds(at, n)]


def trunk(nc, xT, w_ff, w_attn, w_ao, w_gu, w_dn, w_dt, w_ssm, w_so, ssm_heads, ssm_params, gains, fox_cols,
          rope, lam, subln, outT):
    with ExitStack() as ctx:
        sems = {}

        def S(name):
            if name not in sems:
                sems[name] = ctx.enter_context(nc.semaphore(name))
            return sems[name]

        def sb(name, shape, dt=F32, stack=ctx):
            return stack.enter_context(nc.sbuf_tensor(name, shape, dt))

        x = sb("x", [P, KC * SEQ])
        hT = [sb("hT_hi", [P, KC * SEQ], F32R), sb("hT_lo", [P, KC * SEQ], F32R)]
        raw = [sb(f"w_raw{r}", [P, KC * P]) for r in range(2)]
        w_hi = [sb(f"w_hi{r}", [P, KC * P], F32R) for r in range(2)]
        w_lo = [sb(f"w_lo{r}", [P, KC * P], F32R) for r in range(2)]
        rb = sb("inv_rms", [P, SEQ])
        sq = sb("sq", [P, SEQ])
        acc = sb("sum_sq", [P, SEQ])
        ident = sb("ident", [P, P])
        ones = sb("ones", [P, P])
        gain = sb("gain", [P, 5 * KC])
        eps_c = sb("eps_c", [P, 2])
        causal = sb("causal", [P, P])
        last_row = sb("last_row", [P, P])
        gp = sb("ssm_params_sb", [P, GROUPS * GPW])
        hp = sb("ssm_heads_sb", [SSM_HEADS, 2])

        with ExitStack() as st:
            a = lambda name, shape, dt=F32: sb(name, shape, dt, st)
            ff_w = [a("ff_raw", [P, KC, FOX_HEADS]), a("ff_hi", [P, KC * P], F32R), a("ff_lo", [P, KC * P], F32R)]
            ff_t = [a(f"ff_t{n}", [FOX_HEADS, SEQ]) for n in range(6)]
            ff_ones = a("ff_ones", [FOX_HEADS, SEQ])
            ff_c = [a("ff_c_hi", [FOX_HEADS, SEQ], F32R), a("ff_c_lo", [FOX_HEADS, SEQ], F32R)]
        with ExitStack() as st:
            a = lambda name, shape, dt=F32: sb(name, shape, dt, st)
            yT = [a("yT_hi", [P, KC * SEQ], F32R), a("yT_lo", [P, KC * SEQ], F32R)]
            crow = a("fox_rows", [2, FOX_HEADS * SEQ], F32R)
            qs = {k: [a(f"{k}_q_{p}", [P, SEQ], F32R) for p in ("hi", "lo")] for k in "fd"}
            ks = {k: [a(f"{k}_k_{p}", [P, SEQ], F32R) for p in ("hi", "lo")] for k in "fd"}
            vs = {"f": [[a(f"f_v{m}_{p}", [P, NQB, P], F32R) for p in ("hi", "lo")] for m in range(2)]}
            vs["d"] = [[a(f"d_v_{p}", [P, NQB, P], F32R) for p in ("hi", "lo")]]
            vt = a("v_T", [P, SEQ])
            ev = [a(f"evac_{r}", [P, SEQ]) for r in "qk"]
            sw = a("swapped", [P, SEQ])
            rot = a("rotated", [P, SEQ])
            cos = a("cos", [P, SEQ])
            sin = a("sin", [P, SEQ])
            pr = [[a(f"p{par}{m}", [P, SEQ]) for m in range(2)] for par in range(2)]
            pt = [[a(f"pT{m}_{p}", [P, SEQ], F32R) for p in ("hi", "lo")] for m in range(2)]
            negmax = a("negmax", [P, 2, 2])
            rowsum = a("rowsum", [P, 2, 2])
            rinv = a("rinv", [P, 2, 2])
            dsq = a("d_sq", [P, SEQ])
            drs = a("d_rs", [P, SEQ])
            dy = a("d_y", [P, SEQ])
            ones2 = a("ones2", [2, P], F32R)
            ident_r = a("ident_r", [P, P], F32R)
            negmask = a("negmask", [P, P])
            negmask_r = a("negmask_r", [P, P], F32R)
            lamt = a("lam_t", [P, 4, HD])
            lamp = a("lam_p", [P, 2, HD])
            lams = a("lam_s", [P, 4])
            neglam = a("neglam", [P, 1])
            sublnw = a("subln_w", [P, 1])
            bff = a("b_forget", [FOX_HEADS, 1])
        with ExitStack() as st:
            a = lambda name, shape, dt=F32: sb(name, shape, dt, st)
            act = [a("act_hi", [P, FC * SEQ], F32R), a("act_lo", [P, FC * SEQ], F32R)]
            fz = a("ffn_z", [P, SEQ])
            ft = a("ffn_t", [P, SEQ])
            fs = a("ffn_silu", [P, SEQ])
            fu = a("ffn_up", [P, SEQ])
            fa = a("ffn_act", [P, SEQ])

        with ExitStack() as st:
            a = lambda name, shape, dt=F32: sb(name, shape, dt, st)
            a("below_dt", [P, 2 * FC * SEQ + 5 * SEQ])
            dt_w = [a("dt_raw", [P, KC, SSM_HEADS]), a("dt_hi", [P, KC * P], F32R), a("dt_lo", [P, KC * P], F32R)]
        with ExitStack() as st:
            a = lambda name, shape, dt=F32: sb(name, shape, dt, st)
            dt_t = [a(f"dt_t{n}", [SSM_HEADS, SEQ]) for n in range(6)]
            acol = a("A_col", [SSM_HEADS, 1])
            acsT = a("acs_T", [P, NQB * SSM_HEADS])
            decT = a("dec_T", [P, NQB * SSM_HEADS])
        NH4 = NQB * SSM_HEADS
        with ExitStack() as st:
            a = lambda name, shape, dt=F32: sb(name, shape, dt, st)
            gT = a("gated_T", [P, 2 * GROUPS * SEQ])
            ub = [a(f"u{j}", [P, SEQ + 3]) for j in range(4)]
            xs = [a(f"xs{j}", [P, SEQ]) for j in range(4)]
            bc = [[a(f"{n}_{p}", [P, SEQ], F32R) for p in ("hi", "lo")] for n in ("B", "C")]
            zc = [a(f"z{t}", [P, SEQ]) for t in range(2)]
            tt = [a(f"tanh{t}", [P, SEQ]) for t in range(2)]
            ab = a("acs_rows", [P, HPG * SEQ])
            ea = [a(f"exp_acs{t}", [P, SEQ]) for t in range(2)]
            cbm = a("cb_masked", [P, SEQ])
            xst = a("x_dt", [P, NQB, 2 * P])
            xp = [[a(f"xp{r}_{p}", [P, NQB, P], F32R) for p in ("hi", "lo")] for r in range(HPG)]
            xd = [a(f"xd_{p}", [P, 3, 2 * P], F32R) for p in ("hi", "lo")]
            bt = [a(f"b_tok_{p}", [P, 3 * P], F32R) for p in ("hi", "lo")]
            mm_ = [[a(f"m{r}_{p}", [P, SEQ], F32R) for p in ("hi", "lo")] for r in range(2)]
            state = [a(f"state{c}", [P, 2 * P]) for c in range(2)]
            prev = [a(f"prev_{p}", [P, 3 * 2 * P], F32R) for p in ("hi", "lo")]
            rg = sq
            nacs = a("neg_acs_T", [P, NH4])
            dtT = a("dt_T", [P, NH4])
            dsT = a("decay_to_end", [P, NH4])
            cdT = a("chunk_decay", [P, NH4])
        with ExitStack() as st:
            a = lambda name, shape, dt=F32: sb(name, shape, dt, st)
            a("under_gated_T", [P, 2 * GROUPS * SEQ])
            gs = [a(f"gated_{p}", [P, 2 * GROUPS * SEQ], F32R) for p in ("hi", "lo")]

        acs_dram = nc.dram_tensor("acs_dram", [SSM_HEADS, SEQ], F32, kind="Internal").ap()
        rows_dram = nc.dram_tensor("rows_dram", [2 * FOX_HEADS, SEQ], F32, kind="Internal").ap()
        bank = [ctx.enter_context(nc.psum_tensor(f"bank{b}", [P, SEQ], F32)) for b in range(8)]
        GB = bank[0:2]
        SB = bank[2:4]
        TB = bank[4:6]
        OB = bank[6]
        XB = bank[7]

        LAST_DVE, LAST_POOL = (7, 0, 1, 2, 3), (4, 5, 6)

        def last_norm(engine, chunks, done):
            engine.wait_ge(S("rb"), 5)
            engine.wait_ge(S("x_scaled"), KC - 1)
            for c in chunks:
                if c == KC - 1:
                    last = engine.scalar_tensor_tensor(out=columns(x, c), in0=columns(x, c),
                                                       scalar=columns(gain, 4 * KC + c, 1), in1=rb[:],
                                                       op0=ALU.mult, op1=ALU.mult)
                else:
                    last = engine.tensor_tensor(columns(x, c), columns(x, c), rb[:], ALU.mult)
                last.then_inc(S(done), 1)

        block = ctx.enter_context(nc.Block())

        @block.sync
        def _(sp):
            sp.dma_start(columns(x, 0), xT[0]).then_inc(S("x_in0"), 16)
            sp.dma_start(gain[:], gains).then_inc(S("gain_in"), 16)
            sp.dma_start(ff_w[0][:], w_ff).then_inc(S("ff_in"), 16)

            def load(T, r, src, blocks=KC):
                sp.wait_ge(S("w_lo"), T + 1)
                sp.dma_start(raw[r][:, 0:blocks * P], src).then_inc(S(f"w_in{r}"), 16)

            load(T_ATTN, 0, w_attn[0:P, :])
            sp.dma_start(columns(x, 1), xT[1]).then_inc(S("x_in1"), 16)
            load(T_ATTN + 1, 1, w_attn[P:2 * P, :])
            for c in range(2, KC):
                sp.dma_start(columns(x, c), xT[c]).then_inc(S(f"x_in{c}"), 16)
            for dst, src in ((lamt, lam.partition_broadcast(P)), (sublnw, subln), (bff, fox_cols),
                             (cos, rope[0]), (sin, rope[1]), (gp, ssm_params), (hp, ssm_heads)):
                sp.dma_start(dst[:], src).then_inc(S("small_in"), 16)
            for j in range(2, 6):
                load(T_ATTN + j, j % 2, w_attn[j * P:(j + 1) * P, :])
            sp.wait_ge(S("ff_rows"), 2)
            for part in range(2):
                sp.dma_start(rows_dram[part * FOX_HEADS:(part + 1) * FOX_HEADS, :],
                             ff_c[part][:].bitcast(F32)).then_inc(S("rows_stored"), 16)
            sp.wait_ge(S("rows_stored"), 32)
            sp.dma_start(crow[:].bitcast(F32), rows_dram.rearrange("(o h) n -> o (h n)", o=2))\
                .then_inc(S("crow_in"), 16)
            with sp.Fori(1, UNITS) as i:
                for j in range(6):
                    load(T_ATTN + 6 * i + j, j % 2, w_attn[bass.ds((6 * i + j) * P, P), :])
            with sp.Fori(0, KC // 2) as i:
                for j in range(2):
                    load(T_AO + 2 * i + j, j, w_ao[bass.ds((2 * i + j) * P, P), :])
            def ffn_loads(l):
                with sp.Fori(0, FC) as i:
                    for j in range(2):
                        load(T_GU[l] + 2 * i + j, j, w_gu[l][bass.ds((2 * i + j) * P, P), :])
                if l == 0:
                    sp.wait_ge(S("x_add"), KC)
                    sp.dma_start(dt_w[0][:], w_dt).then_inc(S("dt_in"), 16)
                with sp.Fori(0, KC // 2) as i:
                    for j in range(6):
                        m, cut = j // 3, j % 3
                        load(T_DN[l] + 6 * i + j, j % 2,
                             w_dn[l][bass.ds((2 * i + m) * P, P), sum(DOWN_CUT[:cut]) * P:sum(DOWN_CUT[:cut + 1]) * P],
                             DOWN_CUT[cut])

            ffn_loads(0)
            def ssm_loads(g):
                for j in range(6):
                    load(T_SSM + 6 * g + j, j % 2, w_ssm[bass.ds((6 * g + j) * P, P), :])

            def acs_rows(g):
                sp.wait_ge(S("m_lo"), HPG * g + 1)
                src = acs_dram[bass.ds(HPG * g, HPG), :].rearrange("h n -> (h n)").partition_broadcast(P)
                sp.dma_start(ab[:], src).then_inc(S("ab_in"), 16)

            ssm_loads(0)
            sp.wait_ge(S("acs_stored"), 16)
            acs_rows(0)
            with sp.Fori(1, GROUPS) as g:
                ssm_loads(g)
                acs_rows(g)
            with sp.Fori(0, KC // 2) as i:
                for j in range(4):
                    load(T_SO + 4 * i + j, j % 2,
                         w_so[bass.ds((2 * i + j % 2) * P, P), (j // 2) * DM:(j // 2 + 1) * DM])
            ffn_loads(1)
            for n, c in ((0, 7), (0, 4), (1, 0), (2, 1), (1, 5), (3, 2), (4, 3), (2, 6)):
                sp.wait_ge(S("y_out" if c in LAST_DVE else "y_out_pool"), n + 1)
                sp.dma_start(outT[c], columns(x, c)).then_inc(S("stored"), 16)
            sp.wait_ge(S("stored"), 16 * KC)

        @block.gpsimd
        def _(pool):
            pool.nop().then_inc(S("w_lo"), 2)
            pool.nop().then_inc(S("m_lo"), 1)
            for part in (1, 2):
                pool.memset(ff_w[part][:].bitcast(F32), 0.0).then_inc(S("ff_zero"), 1)
            pool.memset(ident[:], 0.0).then_inc(S("c_set"), 1)
            pool.memset(ones[:], 1.0).then_inc(S("c_set"), 1)
            pool.memset(negmask[:], 0.0).then_inc(S("c_set"), 1)
            pool.wait_ge(S("c_set"), 3)
            pool.affine_select(out=ident[:], in_=ident[:], compare_op=ALU.not_equal, fill=1.0, base=0,
                               pattern=[[-1, P]], channel_multiplier=1).then_inc(S("consts"), 1)
            pool.affine_select(out=negmask[:], in_=negmask[:], compare_op=ALU.is_ge, fill=NEG, base=0,
                               pattern=[[-1, P]], channel_multiplier=1).then_inc(S("consts"), 1)
            for m in range(2):
                for part in range(2):
                    pool.memset(vs["f"][m][part][:, :, HD * (1 - m):HD * (2 - m)].bitcast(F32), 0.0)\
                        .then_inc(S("consts"), 1)
            pool.affine_select(out=causal[:], in_=ones[:], compare_op=ALU.is_ge, fill=0.0, base=0,
                               pattern=[[1, P]], channel_multiplier=-1).then_inc(S("consts"), 1)
            pool.affine_select(out=last_row[:], in_=ones[:], compare_op=ALU.is_ge, fill=0.0, base=1 - P,
                               pattern=[[0, P]], channel_multiplier=1).then_inc(S("consts"), 1)

            def lo_parts(start, end):
                with pool.Fori(start // 2, end // 2) as i:
                    for r in range(2):
                        pool.wait_ge(S("w_hi"), 2 * i + r + 1)
                        pool.tensor_tensor(w_lo[r][:], raw[r][:], w_hi[r][:].bitcast(F32), ALU.subtract)\
                            .then_inc(S("w_lo"), 1)

            lo_parts(0, T_DN[0])
            pool.wait_ge(S("x_add"), KC)
            for part in (1, 2):
                pool.memset(dt_w[part][:].bitcast(F32), 0.0).then_inc(S("dt_zero"), 1)
            lo_parts(T_DN[0], T_SSM + 8)

            def ssm_section(g, ahead):
                def w(j):
                    if ahead is not None:
                        T = T_SSM + 6 * ahead + j + 2
                        pool.wait_ge(S("w_hi"), T + 1)
                        pool.tensor_tensor(w_lo[j % 2][:], raw[j % 2][:], w_hi[j % 2][:].bitcast(F32), ALU.subtract)\
                            .then_inc(S("w_lo"), 1)

                def early_lo(c0, c1):
                    for c in range(c0, c1 if ahead is None else c0):
                        pool.wait_ge(S("early_hi"), c + 1)
                        pool.tensor_tensor(columns(hT[1], c), columns(gT, c), columns(hT[0], c).bitcast(F32),
                                           ALU.subtract).then_inc(S("early_lo"), 1)

                def m_lo(r):
                    pool.wait_ge(S("m_hi"), HPG * g + r + 1)
                    pool.tensor_tensor(mm_[r % 2][1][:], ab[:, r * SEQ:(r + 1) * SEQ], mm_[r % 2][0][:].bitcast(F32),
                                       ALU.subtract).then_inc(S("m_lo"), 1)
                w(0)
                early_lo(0, 2)
                m_lo(0)
                early_lo(2, 4)
                m_lo(1)
                w(1)
                w(2)
                early_lo(4, 6)
                m_lo(2)
                m_lo(3)
                early_lo(6, KC)
                w(3)
                w(4)
                pool.wait_ge(S("g_sq"), 2 * g + 2)
                pool.tensor_tensor(sq[:], sq[:], acc[:], ALU.add).then_inc(S("g_sq_sum"), 1)
                w(5)

            with pool.Fori(0, GROUPS - 1) as g:
                ssm_section(g, g + 1)
            ssm_section(GROUPS - 1, None)
            lo_parts(T_SO + 2, T_ALL)
            last_norm(pool, LAST_POOL, "y_out_pool")

        @block.tensor
        def _(pe):
            def hilo(out, lhs, rhs, first, last, lcut, rcut):
                for n, (u, v) in enumerate(((0, 0), (0, 1), (1, 0))):
                    mm = pe.matmul(out, lcut(lhs[u]), rcut(rhs[v]), start=first and n == 0, stop=last and n == 2)
                return mm

            def wblocks(T, G, r, g, rhs, kcs, k0, n_all, rcut):
                if kcs[0] == 0:
                    pe.wait_ge(S("w_lo"), T + 3)
                    if k0 == 0:
                        pe.wait_ge(S("g_out"), G + 1)
                for kc in kcs:
                    mm = hilo(GB[g][:], (w_hi[r], w_lo[r]), rhs, k0 + kc == 0, k0 + kc == n_all - 1,
                              lambda t: t[:, kc * P:(kc + 1) * P], lambda t: rcut(t, k0 + kc))
                return mm

            chunk = columns

            def first_tile(T, G, n):
                for kc in range(KC):
                    pe.wait_ge(S("h_lo"), KC * n + kc + 1)
                    mm = wblocks(T, G, 0, 0, hT, [kc], 0, KC, chunk)
                mm.then_inc(S("tile_done"), 1)
                sum_squares(n)

            def sum_squares(n):
                pe.wait_ge(S("sq_sum"), KC * (n + 1) + 1)
                pe.matmul(XB[:], ones[:], acc[:], start=True, stop=True).then_inc(S("ms"), 1)

            for name, credit in (("tile_done", 2), ("v_turned", 1), ("turned", 2), ("pv", 5), ("s", 9),
                                 ("y_diag", 1), ("y_off", 2), ("state_mm", 1), ("g_ms", 1),
                                 ("b_turned", 1)):
                pe.nop().then_inc(S(name), credit)
            pe.wait_ge(S("consts"), 8)
            pe.wait_ge(S("ff_w_lo"), 1)
            for kc in range(KC):
                pe.wait_ge(S("h_lo"), kc + 1)
                ff = hilo(OB[:], ff_w[1:3], hT, kc == 0, kc == KC - 1,
                          lambda t: t[:, kc * P:(kc + 1) * P], lambda t: columns(t, kc))
                mm = wblocks(T_ATTN, G_ATTN, 0, 0, hT, [kc], 0, KC, chunk)
            ff.then_inc(S("ff_mm"), 1)
            mm.then_inc(S("tile_done"), 1)
            sum_squares(0)

            def gemm(k, u, c):
                j = c // 4 + 3 * (k == "d")
                T = T_ATTN + 6 * u + j
                mm = wblocks(T, T, j % 2, j % 2, hT, [2 * (c % 4), 2 * (c % 4) + 1], 0, KC, chunk)
                if c % 4 == 3:
                    mm.then_inc(S("tile_done"), 1)

            def v_turn(k, u):
                n = 2 * u + (k == "d")
                pe.wait_ge(S("g_out"), 6 * u + 3 * (k == "d") + 3)
                pe.wait_ge(S("v_lo"), n + 1)
                if k == "d":
                    pe.wait_ge(S("d_ln"), u + 1)
                elif not isinstance(u, int):
                    pe.wait_ge(S("d_ln"), u)
                for b in range(NQB):
                    mm = pe.transpose(XB[:, b * P:(b + 1) * P], vt[:, b * P:(b + 1) * P], ident[:])
                mm.then_inc(S("v_turned"), 1)

            def scores(k, u, s):
                n, N = 2 * u + (k == "d"), (s + 1) * P
                if s == 0:
                    pe.wait_ge(S("q_lo"), n + 2)
                    pe.wait_ge(S("k_lo"), n + 2)
                for m in range(2):
                    pe.wait_ge(S("exp"), 8 * n + 2 * s + m + 1)
                    row = slice(HD * m, HD * m + HD)
                    out = SB[m][:, 0:N]
                    hilo(out, qs[k], ks[k], True, False,
                         lambda t: t[row, s * P:(s + 1) * P], lambda t: t[row, 0:N])
                    if k == "f":
                        if m == 0 and s == 0:
                            pe.wait_ge(S("crow_in"), 16)
                        pe.matmul(out, ones2[:], width_at(crow, (2 * u + m) * SEQ, N), start=False, stop=False)
                    pe.matmul(SB[m][:, s * P:N], ident_r[:], negmask_r[:], start=False, stop=True)\
                        .then_inc(S("s"), 1)

            def turn(k, u, s):
                n = 2 * u + (k == "d")
                pe.wait_ge(S("p"), 4 * n + s + 1)
                for m in range(2 if k == "f" else 1):
                    for b in range(s + 1):
                        mm = pe.transpose(TB[m][:, b * P:(b + 1) * P], pr[s % 2][m][:, b * P:(b + 1) * P], ident[:])
                mm.then_inc(S("turned"), 1)

            def pv(k, u, s):
                n = 2 * u + (k == "d")
                pe.wait_ge(S("pT_lo"), 4 * n + s + 1)
                if s == 0:
                    pe.wait_ge(S("v_lo"), n + 2)
                    pe.wait_ge(S("o_out"), n + 1)
                maps = 2 if k == "f" else 1
                for m in range(maps):
                    for b in range(s + 1):
                        mm = hilo(OB[:, s * P:(s + 1) * P], vs[k][m], pt[m], m == 0 and b == 0,
                                  m == maps - 1 and b == s,
                                  lambda t: t[:, b, :], lambda t: t[:, b * P:(b + 1) * P])
                mm.then_inc(S("pv"), 1)

            def sub_ms(u, v_loaded):
                pe.wait_ge(S("d_sq"), u + 1)
                pe.wait_ge(S("v_lo"), v_loaded)
                pe.matmul(XB[:], ones[:], dsq[:], start=True, stop=True).then_inc(S("d_ms"), 1)

            def out_first(c):
                order = (0, 1, 2, 4, 5, 6, 3)
                n = c % 6
                for kc in order[n:n + 1] if n < 5 else order[5:]:
                    if n == 0:
                        pe.wait_ge(S("o_out"), 2 * UNITS - 1)
                        pe.wait_ge(S("dy_lo"), UNITS)
                    if kc == 3:
                        pe.wait_ge(S("o_out"), 2 * UNITS)
                    wblocks(T_AO + c // 6, G_AO + c // 6, c // 6, c // 6, yT, [kc], 0, KC, chunk)

            def section(att, proj):
                kg = iter(range(12))

                def g(quarters=2):
                    for _ in range(quarters):
                        if proj:
                            gemm(*proj, next(kg))
                        else:
                            out_first(next(kg))
                g(3)
                scores(*att, 0)
                g(1)
                scores(*att, 1)
                turn(*att, 0)
                g(2)
                pv(*att, 0)
                if proj:
                    v_turn(*proj)
                scores(*att, 2)
                turn(*att, 1)
                g(2)
                pv(*att, 1)
                scores(*att, 3)
                g(1)
                turn(*att, 2)
                g(2)
                pv(*att, 2)
                turn(*att, 3)
                g(1)
                pv(*att, 3)
                if att[0] == "d":
                    sub_ms(att[1], 2 * att[1] + (4 if proj else 3))

            for c in range(4, 12):
                gemm("f", 0, c)
            pe.wait_ge(S("ln"), 1)
            v_turn("f", 0)
            with pe.Fori(0, UNITS - 1) as i:
                section(("f", i), ("d", i))
                section(("d", i), ("f", i + 1))
            section(("f", UNITS - 1), ("d", UNITS - 1))
            section(("d", UNITS - 1), None)

            pe.wait_ge(S("o_out"), 2 * UNITS + 1)
            pe.wait_ge(S("dy_lo"), UNITS + 1)
            for j in range(2):
                wblocks(T_AO + j, G_AO + j, j, j, yT, [KC - 1], 0, KC, chunk).then_inc(S("tile_done"), 1)
            with pe.Fori(1, KC // 2) as i:
                for j in range(2):
                    T, G = T_AO + 2 * i + j, G_AO + 2 * i + j
                    wblocks(T, G, j, j, yT, range(KC), 0, KC, chunk).then_inc(S("tile_done"), 1)
            def ffn(l, norm):
                first_tile(T_GU[l], G_GU[l], norm - 1)
                wblocks(T_GU[l] + 1, G_GU[l] + 1, 1, 1, hT, range(KC), 0, KC, chunk).then_inc(S("tile_done"), 1)
                with pe.Fori(1, FC) as i:
                    for j in range(2):
                        wblocks(T_GU[l] + 2 * i + j, G_GU[l] + 2 * i + j, j, j, hT, range(KC), 0, KC, chunk)\
                            .then_inc(S("tile_done"), 1)
                with pe.Fori(0, KC // 2) as i:
                    for j in range(6):
                        m, cut = j // 3, j % 3
                        pe.wait_ge(S("act_lo"), FC * l + sum(DOWN_CUT[:cut + 1]))
                        wblocks(T_DN[l] + 6 * i + j, G_DN[l] + 2 * i + m, j % 2, m, act, range(DOWN_CUT[cut]),
                                sum(DOWN_CUT[:cut]), FC, chunk).then_inc(S("tile_done"), 1)

            ffn(0, 2)

            CB, TR, STB, YD, YO, NX = SB[0], SB[1], TB[0], TB[1], OB, XB
            first_tile(T_SSM, G_SSM, 2)
            pe.wait_ge(S("dt_w_lo"), 1)
            for kc in range(KC):
                mm = hilo(CB[:], dt_w[1:3], hT, kc == 0, kc == KC - 1,
                          lambda t: t[:, kc * P:(kc + 1) * P], lambda t: columns(t, kc))
            mm.then_inc(S("dt_mm"), 1)

            def front(g, j, halves=(0, 1)):
                T = T_SSM + 6 * g + j
                for h in halves:
                    mm = wblocks(T, G_SSM + 6 * g + j, j % 2, j % 2, hT, range(h * KC // 2, (h + 1) * KC // 2), 0, KC,
                                 chunk)
                if h == 1:
                    mm.then_inc(S("tile_done"), 1)

            def blk(t, c):
                return t[:, c * P:(c + 1) * P]

            def cb_and_turns(g):
                pe.wait_ge(S("bc_lo"), 2 * g + 3)
                pe.wait_ge(S("cb_masked"), g + 1)
                for c in range(NQB):
                    mm = hilo(blk(CB, c), bc[0], bc[1], True, True, lambda t: blk(t, c), lambda t: blk(t, c))
                mm.then_inc(S("cb"), 1)
                pe.wait_ge(S("y_sum"), 2 * g + 1)
                for b, src, n, name in ((TR, xs[0], 4, "x0_turned"), (YD, xs[1], 4, "x1_turned"),
                                        (YO, xs[2], 3, "b_turned")):
                    for c in range(n):
                        mm = pe.transpose(blk(b, c), blk(src, c), ident[:])
                    mm.then_inc(S(name), 1)

            def chunk_state(g, c):
                if c == 0:
                    pe.wait_ge(S("xd_lo"), g + 2)
                    pe.wait_ge(S("bt_lo"), g + 1)
                pe.wait_ge(S("state_out"), 3 * g + (3 if c == 2 else 1))
                hilo(STB[:, (c % 2) * 2 * P:(c % 2 + 1) * 2 * P], bt, xd, True, True,
                     lambda t: blk(t, c), lambda t: t[:, c, :]).then_inc(S("state_mm"), 1)

            def y_diag(g, t):
                if t == 0:
                    pe.wait_ge(S("xp_lo"), g + 1)
                else:
                    pe.wait_ge(S("y_sum"), 2 * g + 2)
                pe.wait_ge(S("m_lo"), HPG * g + 2 * t + 3)
                for c in range(NQB):
                    for r in range(2):
                        mm = hilo(blk(YD, c), xp[2 * t + r], mm_[r], r == 0, r == 1,
                                  lambda w: w[:, c, :], lambda w: blk(w, c))
                mm.then_inc(S("y_diag"), 1)

            def y_off(g, t):
                pe.wait_ge(S("prev_lo"), 3 * g + 3)
                for c in range(1, NQB):
                    mm = hilo(blk(YO, c), prev, bc[1], True, True,
                              lambda w: blk(w, 2 * (c - 1) + t), lambda w: blk(w, c))
                mm.then_inc(S("y_off"), 1)

            def group_ms(g):
                pe.wait_ge(S("g_sq_sum"), g + 1)
                pe.wait_ge(S("g_ln"), g + 1)
                pe.matmul(NX[:], ones[:], sq[:], start=True, stop=True).then_inc(S("g_ms"), 1)

            def so_early(m, part):
                for kc in range(part * KC // 2, (part + 1) * KC // 2):
                    pe.wait_ge(S("early_lo"), kc + 1)
                    mm = wblocks(T_SO + m, G_SO + m, m, m, hT, [kc], 0, 2 * KC, chunk)
                if part == 1:
                    mm.then_inc(S("tile_done"), 1)

            def ssm_section(back, ahead):
                def f(j, halves=(0, 1)):
                    if ahead is not None:
                        front(ahead, j, halves)

                def early(m, part):
                    if ahead is None:
                        so_early(m, part)
                f(0)
                if not (isinstance(back, int) and back == 0):
                    group_ms(back - 1)
                cb_and_turns(back)
                f(1)
                early(0, 0)
                f(2)
                chunk_state(back, 0)
                chunk_state(back, 1)
                y_diag(back, 0)
                f(3, (0,))
                chunk_state(back, 2)
                early(0, 1)
                f(3, (1,))
                y_off(back, 0)
                f(4)
                early(1, 0)
                y_diag(back, 1)
                y_off(back, 1)
                f(5)
                early(1, 1)

            for j in range(1, 4):
                front(0, j)
            pe.wait_ge(S("acs"), 1)
            for c in range(NQB):
                pe.transpose(TR[:, c * SSM_HEADS:(c + 1) * SSM_HEADS], dt_t[4][:, c * P:(c + 1) * P],
                             ident[0:SSM_HEADS, 0:SSM_HEADS])
                mm = pe.transpose(TR[:, NH4 + c * SSM_HEADS:NH4 + (c + 1) * SSM_HEADS],
                                  dt_t[3][:, c * P:(c + 1) * P], ident[0:SSM_HEADS, 0:SSM_HEADS])
            mm.then_inc(S("acs_turned"), 1)
            front(0, 4, (0,))
            pe.wait_ge(S("acs_T"), 1)
            pe.matmul(YD[:, 0:NH4], last_row[:], acsT[:], start=True, stop=True).then_inc(S("acs_end"), 1)
            front(0, 4, (1,))
            front(0, 5)
            ssm_section(0, 1)
            with pe.Fori(1, GROUPS - 1) as g:
                ssm_section(g, g + 1)
            ssm_section(GROUPS - 1, None)
            group_ms(GROUPS - 1)

            def so(i, js):
                for j in js:
                    half, m = j // 2, j % 2
                    wblocks(T_SO + 4 * i + j, G_SO + 2 * i + m, m, m, gs, range(KC), half * KC, 2 * KC, chunk)\
                        .then_inc(S("tile_done"), 1)

            for m in range(2):
                for kc in range(KC):
                    pe.wait_ge(S("gs_lo"), kc + 1)
                    mm = wblocks(T_SO + 2 + m, G_SO + m, m, m, gs, [kc], KC, 2 * KC, chunk)
                mm.then_inc(S("tile_done"), 1)
            pe.wait_ge(S("gs_lo"), 2 * KC)
            with pe.Fori(1, KC // 2) as i:
                so(i, range(4))

            ffn(1, 4)
            sum_squares(4)

        @block.scalar
        def _(act_e):
            def w_hi_part(T, half, r):
                act_e.wait_ge(S(f"w_in{r}"), 16 * (half + 1))
                act_e.wait_ge(S("tile_done"), T + 1)
                act_e.activation(w_hi[r][:], raw[r][:], ACT.Copy).then_inc(S("w_hi"), 1)

            def inv_rms(n):
                act_e.wait_ge(S("ms"), n + 1)
                act_e.activation(sq[:], XB[:], ACT.Ln, bias=eps_c[:, 0:1], scale=1.0 / DM).then_inc(S("ln"), 1)
                act_e.wait_ge(S("ln"), n + 1)
                act_e.activation(rb[:], sq[:], ACT.Exp, scale=-0.5).then_inc(S("rb"), 1)

            def apart():
                act_e.sem_inc(S("act_waited"), 1)

            def x_chunk(R, c, n, keep=True):
                apart()
                if keep:
                    act_e.activation(columns(hT[0], c), columns(x, c), ACT.Copy,
                                     scale=columns(gain, n * KC + c, 1)).then_inc(S("h_hi"), 1)
                act_e.wait_ge(S("sq_sum"), R + 1)
                apart()
                act_e.activation(sq[:], columns(x, c), ACT.Square).then_inc(S("sq"), 1)
                if not keep and not (isinstance(c, int) and c == KC - 1):
                    act_e.wait_ge(S("sq"), R + 1)
                    apart()
                    act_e.activation(columns(x, c), columns(x, c), ACT.Copy, scale=columns(gain, n * KC + c, 1))\
                        .then_inc(S("x_scaled"), 1)

            act_e.nop().then_inc(S("exp"), 2)
            act_e.nop().then_inc(S("d_ln"), 1)
            act_e.wait_ge(S("ff_in"), 16)
            act_e.wait_ge(S("ff_zero"), 2)
            act_e.activation(first_columns(ff_w[1], FOX_HEADS), ff_w[0][:], ACT.Copy).then_inc(S("ff_w_hi"), 1)
            act_e.wait_ge(S("gain_in"), 16)
            for c in range(KC):
                act_e.wait_ge(S(f"x_in{c}"), 16)
                x_chunk(c, c, 0)
                if c < 2:
                    w_hi_part(c, 0, c)
            w_hi_part(2, 1, 0)
            act_e.wait_ge(S("setup"), 5)
            inv_rms(0)
            act_e.wait_ge(S("lam"), 2)
            act_e.activation(lams[:, 2:4], lams[:, 0:2], ACT.Exp).then_inc(S("lam_exp"), 1)
            act_e.wait_ge(S("ff_abs"), 1)
            act_e.activation(ff_t[2][:], ff_t[1][:], ACT.Exp, scale=-1.0).then_inc(S("ff_exp"), 1)
            def exps(n, s):
                N = (s + 1) * P
                for m in range(2):
                    act_e.wait_ge(S("max"), 8 * n + 2 * s + m + 1)
                    act_e.wait_ge(S("turned"), 4 * n + s + 1)
                    act_e.activation(pr[s % 2][m][:, 0:N], SB[m][:, 0:N], ACT.Exp, bias=negmax[:, s % 2, m:m + 1],
                                     accum_out=rowsum[:, s % 2, m:m + 1]).then_inc(S("exp"), 1)

            def p_hi(k, n, s):
                N = (s + 1) * P
                act_e.wait_ge(S("turned"), 4 * n + s + 3)
                for m in range(2 if k == "f" else 1):
                    last = act_e.activation(pt[m][0][:, 0:N], TB[m][:, 0:N], ACT.Copy)
                last.then_inc(S("pT_hi"), 1)

            def v_hi(k, n):
                act_e.wait_ge(S("v_turned"), n + 2)
                act_e.wait_ge(S("pv"), 4 * n + 1)
                turned = XB[:].rearrange("p (b d) -> p b d", d=P)
                if k == "f":
                    for m in range(2):
                        half = slice(HD * m, HD * (m + 1))
                        last = act_e.activation(vs[k][m][0][:, :, half], turned[:, :, half], ACT.Copy)
                else:
                    last = act_e.activation(vs[k][0][0][:], turned, ACT.Copy)
                last.then_inc(S("v_hi"), 1)

            def swap(u, r, T):
                act_e.wait_ge(S("g_out"), T + 3)
                act_e.wait_ge(S("rope_b"), 2 * u + r + 1)
                for m in range(4):
                    to, of = 32 * (m ^ 1), 32 * m
                    last = act_e.activation(sw[to:to + 32, :], ev[r][of:of + 32, :], ACT.Copy)
                last.then_inc(S("swapped"), 1)

            def qk_hi(k, u, n, r, T):
                if k == "d":
                    act_e.wait_ge(S("rope"), 2 * u + r + 2)
                else:
                    act_e.wait_ge(S("g_out"), T + 3)
                act_e.wait_ge(S("s"), 8 * n + 1)
                act_e.activation((qs, ks)[r][k][0][:], ev[r][:], ACT.Copy).then_inc(S("qk"[r] + "_hi"), 1)

            def out_hi(k, u, n):
                act_e.wait_ge(S("pv"), 4 * n + 9)
                if k == "f":
                    apart()
                    act_e.activation(columns(yT[0], u), OB[:], ACT.Copy).then_inc(S("y_hi"), 1)
                    return
                act_e.activation(dsq[:], OB[:], ACT.Square).then_inc(S("d_sq"), 1)
                act_e.wait_ge(S("d_ms"), u + 1)
                act_e.wait_ge(S("o_out"), n)
                act_e.activation(drs[:], XB[:], ACT.Ln, bias=eps_c[:, 0:1], scale=1.0 / P).then_inc(S("d_ln"), 1)
                act_e.wait_ge(S("d_ln"), u + 2)
                act_e.activation(drs[:], drs[:], ACT.Exp, scale=-0.5).then_inc(S("d_rs"), 1)
                act_e.wait_ge(S("o_out"), n + 2)
                apart()
                act_e.activation(columns(yT[0], u + UNITS), dy[:], ACT.Copy).then_inc(S("y_hi"), 1)

            def section(att, proj):
                if proj:
                    kp, up = proj
                    np_, j0 = 2 * up + (kp == "d"), 3 * (kp == "d")
                    T0 = T_ATTN + 6 * up + j0

                def w(j):
                    if proj:
                        jj = j0 + j + 2
                        w_hi_part(T0 + j + 2, T_ATTN // 2 + 3 * up + jj // 2, jj % 2)

                def qk(r):
                    if proj:
                        qk_hi(kp, up, np_, r, T0 + 1 + r)

                def qk_swap(r):
                    if proj and kp == "d":
                        swap(up, r, T0 + 1 + r)
                k, u = att
                n = 2 * u + (k == "d")
                exps(n, 0)
                w(0)
                exps(n, 1)
                p_hi(k, n, 0)
                if proj:
                    v_hi(kp, np_)
                exps(n, 2)
                p_hi(k, n, 1)
                w(1)
                qk_swap(0)
                exps(n, 3)
                qk(0)
                p_hi(k, n, 2)
                p_hi(k, n, 3)
                w(2)
                qk_swap(1)
                qk(1)
                out_hi(k, u, n)

            w_hi_part(3, 1, 1)
            qk_hi("f", 0, 0, 0, T_ATTN + 1)
            w_hi_part(4, 2, 0)
            v_hi("f", 0)
            qk_hi("f", 0, 0, 1, T_ATTN + 2)
            with act_e.Fori(0, UNITS - 1) as i:
                section(("f", i), ("d", i))
                section(("d", i), ("f", i + 1))
            section(("f", UNITS - 1), ("d", UNITS - 1))
            section(("d", UNITS - 1), None)

            def residual(T, R, c, n, keep=True):
                act_e.wait_ge(S("x_add"), R - KC + 1)
                x_chunk(R, c, n, keep)

            with act_e.Fori(0, KC // 2) as i:
                for j in range(2):
                    w_hi_part(T_AO + 2 * i + j + 2, T_AO // 2 + i + 1, j)
                    if j == 0:
                        act_e.wait_ge(S("rb"), 1)
                    residual(T_AO + 2 * i + j, RES_AO + 2 * i + j, 2 * i + j, 1)
            inv_rms(1)

            def ffn(l, R, norm):
                with act_e.Fori(0, FC) as i:
                    w_hi_part(T_GU[l] + 2 * i + 2, T_GU[l] // 2 + i + 1, 0)
                    act_e.wait_ge(S("ffn_z"), FC * l + i + 1)
                    act_e.activation(ft[:], fz[:], ACT.Tanh).then_inc(S("ffn_tanh"), 1)
                    w_hi_part(T_GU[l] + 2 * i + 3, T_GU[l] // 2 + i + 1, 1)
                    act_e.wait_ge(S("ffn_act"), FC * l + i + 1)
                    apart()
                    act_e.activation(columns(act[0], i), fa[:], ACT.Copy).then_inc(S("act_hi"), 1)
                last = l == 1
                if l == 0:
                    act_e.wait_ge(S("dt_in"), 16)
                    act_e.wait_ge(S("dt_zero"), 2)
                    act_e.activation(first_columns(dt_w[1], SSM_HEADS), dt_w[0][:], ACT.Copy)\
                        .then_inc(S("dt_w_hi"), 1)

                def down(i, final):
                    for j in range(6):
                        T = T_DN[l] + 6 * i + j
                        if not (final and j >= 4):
                            w_hi_part(T + 2, T_DN[l] // 2 + 3 * i + j // 2 + 1, j % 2)
                        if j == 0:
                            act_e.wait_ge(S("rb"), norm)
                        if j % 3 == 2:
                            residual(T, R + 2 * i + j // 3, 2 * i + j // 3, norm, not last)
                with act_e.Fori(0, KC // 2 - last) as i:
                    down(i, False)
                if last:
                    down(KC // 2 - 1, True)
                inv_rms(norm)

            ffn(0, RES_DN0, 2)

            CB, TR, STB, YD, YO, NX = SB[0], SB[1], TB[0], TB[1], OB, XB

            def copy(out, in_):
                return act_e.activation(out, in_, ACT.Copy)

            def tanh(n, src, buf, ready, value):
                act_e.wait_ge(S(ready), value)
                act_e.wait_ge(S("silu"), n + 1)
                act_e.activation(tt[buf][:], src[:], ACT.Tanh).then_inc(S("tanh"), 1)

            def w(g, j):
                w_hi_part(T_SSM + 6 * g + j + 2, T_SSM // 2 + 3 * g + j // 2 + 1, j % 2)

            def conv_tanh(g, j):
                tanh(6 * g + j, xs[j], j % 2, "conv", 12 * g + 3 * j + 4)

            def z_tanh(g, t):
                tanh(6 * g + 4 + t, zc[t], t, "g_out", G_SSM + 6 * g + 4 + t + 3)

            def conv_first(g, j):
                act_e.wait_ge(S("g_out"), G_SSM + 6 * g + j + 3)
                act_e.wait_ge(S("b_turned"), g + 1)
                apart()
                act_e.activation(xs[j][:], ub[j][:, 3:], ACT.Identity, bias=columns(gp, g * GPW + 5 * j + 4, 1),
                                 scale=columns(gp, g * GPW + 5 * j + 3, 1)).then_inc(S("conv_first"), 1)

            def bc_hi(g, j):
                act_e.wait_ge(S("silu"), 6 * g + j + 5)
                if j == 1:
                    act_e.wait_ge(S("y_off"), 2 * g + 2)
                copy(bc[j][0][:], xs[2 + j][:]).then_inc(S("bc_hi"), 1)

            act_e.nop().then_inc(S("g_ln"), 1)
            act_e.activation(acol[:], hp[:, 1:2], ACT.Exp).then_inc(S("A_exp"), 1)
            w(0, 0)
            act_e.wait_ge(S("dt_abs"), 1)
            act_e.activation(dt_t[2][:], dt_t[1][:], ACT.Exp, scale=-1.0).then_inc(S("dt_exp"), 1)
            conv_first(0, 0)
            w(0, 1)
            conv_first(0, 1)
            conv_tanh(0, 0)
            w(0, 2)
            act_e.wait_ge(S("acs"), 1)
            act_e.dma_start(acs_dram, dt_t[4][:]).then_inc(S("acs_stored"), 16)
            conv_first(0, 2)
            conv_tanh(0, 1)
            w(0, 3)
            conv_first(0, 3)
            conv_tanh(0, 2)
            bc_hi(0, 0)
            act_e.wait_ge(S("dec_T"), 1)
            act_e.activation(dsT[:], decT[:], ACT.Exp).then_inc(S("decays"), 1)
            act_e.activation(cdT[:], YD[:, 0:NH4], ACT.Exp).then_inc(S("decays"), 1)
            conv_tanh(0, 3)
            w(0, 4)
            bc_hi(0, 1)
            z_tanh(0, 0)
            w(0, 5)
            z_tanh(0, 1)

            def exp_rows(g):
                act_e.wait_ge(S("ab_in"), 16 * (g + 1))
                act_e.wait_ge(S("y_sum"), 2 * g + 1)
                for t in range(2):
                    for h in range(2):
                        half = slice(HD * h, HD * (h + 1))
                        last = act_e.activation(ea[t][half, :], ab[half, (2 * t + h) * SEQ:(2 * t + h + 1) * SEQ],
                                                ACT.Exp)
                last.then_inc(S("ea"), 1)

            def decay_exp(g, r):
                act_e.wait_ge(S("decay_arg"), HPG * g + r + 1)
                cut = ab[:, r * SEQ:(r + 1) * SEQ]
                act_e.activation(cut, cut, ACT.Exp).then_inc(S("decay"), 1)

            def xp_hi(g):
                act_e.wait_ge(S("x_dt"), g + 1)
                act_e.wait_ge(S("y_diag"), 2 * g + 1)
                for r in range(HPG):
                    half = slice(HD * (r % 2), HD * (r % 2 + 1))
                    last = copy(xp[r][0][:, :, half], xst[:, :, HD * r:HD * (r + 1)])
                last.then_inc(S("xp_hi"), 1)

            def m_hi(g, r):
                act_e.wait_ge(S("m"), HPG * g + r + 2)
                act_e.wait_ge(S("y_diag"), 2 * g + r // 2 + 1)
                copy(mm_[r % 2][0][:], ab[:, r * SEQ:(r + 1) * SEQ]).then_inc(S("m_hi"), 1)

            def prev_hi(g, c):
                act_e.wait_ge(S("state_out"), 3 * g + c + 2)
                if c == 0:
                    act_e.wait_ge(S("y_off"), 2 * g + 2)
                copy(prev[0][:, c * 2 * P:(c + 1) * 2 * P], state[c % 2][:]).then_inc(S("prev_hi"), 1)

            def g_square(g, t):
                act_e.wait_ge(S("gated"), 2 * g + t + 3)
                act_e.wait_ge(S("g_ms"), g + 1)
                act_e.wait_ge(S("g_norm"), 2 * g + 1)
                apart()
                act_e.activation((sq, acc)[t][:], columns(gT, 2 * g + t), ACT.Square).then_inc(S("g_sq"), 1)

            def group_rms(g):
                act_e.wait_ge(S("g_ms"), g + 2)
                act_e.activation(rg[:], NX[:], ACT.Ln, bias=eps_c[:, 1:2], scale=1.0 / (2 * P)).then_inc(S("g_ln"), 1)
                act_e.wait_ge(S("g_ln"), g + 2)
                act_e.activation(rg[:], rg[:], ACT.Exp, scale=-0.5).then_inc(S("rg"), 1)

            def ssm_section(g, ahead):
                def wf(j):
                    if ahead is not None:
                        w(ahead, j)

                def tf(j):
                    if ahead is not None:
                        conv_tanh(ahead, j)
                def early_hi(c0, c1):
                    if ahead is None:
                        act_e.wait_ge(S("tile_done"), T_SO + 2)
                        act_e.wait_ge(S("g_norm"), KC + 1)
                        for c in range(c0, c1):
                            copy(columns(hT[0], c), columns(gT, c)).then_inc(S("early_hi"), 1)

                def cf(j):
                    if ahead is not None:
                        conv_first(ahead, j)
                decay_exp(g, 0)
                wf(0)
                decay_exp(g, 1)
                act_e.wait_ge(S("b_turned"), g + 2)
                act_e.wait_ge(S("state_mm"), 3 * g + 1)
                copy(bt[0][:], YO[:, 0:3 * P]).then_inc(S("bt_hi"), 1)
                early_hi(0, 2)
                xp_hi(g)
                m_hi(g, 0)
                early_hi(2, 4)
                cf(0)
                act_e.wait_ge(S("x_decayed"), g + 1)
                copy(xd[0][:], xst[:, 0:3, :]).then_inc(S("xd_hi"), 1)
                m_hi(g, 1)
                wf(1)
                decay_exp(g, 2)
                decay_exp(g, 3)
                cf(1)
                prev_hi(g, 0)
                prev_hi(g, 1)
                if not (isinstance(g, int) and g == 0):
                    group_rms(g - 1)
                tf(0)
                early_hi(4, 6)
                wf(2)
                prev_hi(g, 2)
                m_hi(g, 2)
                m_hi(g, 3)
                early_hi(6, KC)
                cf(2)
                tf(1)
                wf(3)
                g_square(g, 0)
                cf(3)
                wf(4)
                tf(2)
                if ahead is not None:
                    bc_hi(ahead, 0)
                g_square(g, 1)
                wf(5)
                tf(3)
                if ahead is not None:
                    bc_hi(ahead, 1)
                    z_tanh(ahead, 0)
                if ahead is not None:
                    z_tanh(ahead, 1)
                    exp_rows(ahead)
                else:
                    for m in range(2):
                        w_hi_part(T_SO + 2 + m, T_SO // 2 + 1, m)

            exp_rows(0)
            ssm_section(0, 1)
            with act_e.Fori(1, GROUPS - 1) as g:
                ssm_section(g, g + 1)
            ssm_section(GROUPS - 1, None)
            group_rms(GROUPS - 1)

            act_e.wait_ge(S("g_norm"), 2 * GROUPS + 1)
            for c in (*range(KC, 2 * KC), *range(KC)):
                copy(columns(gs[0], c), columns(gT, c)).then_inc(S("gs_hi"), 1)
            def so(i):
                for m in range(2):
                    w_hi_part(T_SO + 4 * i + m + 4, T_SO // 2 + 2 * i + 2, m)
                    residual(T_SO + 4 * i + 2 + m, RES_SO + 2 * i + m, 2 * i + m, 3)

            act_e.wait_ge(S("setup"), 8)
            so(0)
            with act_e.Fori(1, KC // 2) as i:
                for m in range(2):
                    w_hi_part(T_SO + 4 * i + m + 2, T_SO // 2 + 2 * i + 1, m)
                so(i)
            inv_rms(3)

            ffn(1, RES_DN1, 4)

        @block.vector
        def _(dve):
            made = [0]

            def link(ins):
                made[0] += 1
                ins.then_inc(S("dve_step"), 1)
                dve.wait_ge(S("dve_step"), made[0])

            def x_chunk(R, c, n, keep=True):
                if keep:
                    dve.wait_ge(S("h_hi"), R + 1)
                    dve.scalar_tensor_tensor(out=columns(hT[1], c), in0=columns(x, c),
                                             scalar=columns(gain, n * KC + c, 1),
                                             in1=columns(hT[0], c).bitcast(F32), op0=ALU.mult,
                                             op1=ALU.subtract).then_inc(S("h_lo"), 1)
                dve.wait_ge(S("sq"), R + 1)
                dve.wait_ge(S("sq_sum"), R + 1)
                dve.tensor_tensor(acc[:], acc[:], sq[:], ALU.add).then_inc(S("sq_sum"), 1)

            for name, credit in (("g_out", 2), ("v_lo", 1), ("q_lo", 1), ("k_lo", 1), ("rope_b", 1), ("rope", 1),
                                 ("o_out", 1), ("dy_lo", 1), ("sq_sum", 1)):
                dve.nop().then_inc(S(name), credit)
            dve.memset(eps_c[:, 0:1], EPS).then_inc(S("setup"), 1)
            dve.memset(eps_c[:, 1:2], GATED_EPS).then_inc(S("setup"), 1)
            dve.memset(acc[:], 0.0).then_inc(S("setup"), 1)
            link(dve.memset(ff_ones[:], 1.0))
            dve.wait_ge(S("consts"), 8)
            dve.tensor_copy(ident_r[:], ident[:]).then_inc(S("setup"), 1)
            dve.tensor_copy(negmask_r[:], negmask[:]).then_inc(S("setup"), 1)
            dve.tensor_copy(ones2[:], ones[0:2, :]).then_inc(S("setup"), 1)
            dve.wait_ge(S("ff_w_hi"), 1)
            dve.tensor_tensor(first_columns(ff_w[2], FOX_HEADS), ff_w[0][:],
                              first_columns(ff_w[1], FOX_HEADS).bitcast(F32), ALU.subtract).then_inc(S("ff_w_lo"), 1)
            dve.wait_ge(S("gain_in"), 16)
            dve.wait_ge(S("setup"), 6)
            for c in range(KC):
                x_chunk(c, c, 0)
            dve.wait_ge(S("small_in"), 16 * 7)
            for h in range(2):
                link(dve.tensor_tensor(lamp[:, h, :], lamt[:, 2 * h, :], lamt[:, 2 * h + 1, :], ALU.mult))
            for h in range(2):
                dve.tensor_reduce(lams[:, h:h + 1], lamp[:, h, :], AX.X, ALU.add).then_inc(S("lam"), 1)
            link(dve.tensor_scalar(sublnw[:], sublnw[:], 1.0 - LAM_INIT, None, ALU.mult))
            dve.wait_ge(S("lam_exp"), 1)
            link(dve.tensor_tensor(lams[:, 0:1], lams[:, 3:4], lams[:, 2:3], ALU.subtract))
            link(dve.tensor_scalar(neglam[:], lams[:, 0:1], -LAM_INIT, None, ALU.add))

            def softplus_abs(t, abs_done):
                dve.scalar_tensor_tensor(out=t[1][:], in0=t[0][:], scalar=-1.0, in1=t[0][:], op0=ALU.mult,
                                         op1=ALU.max).then_inc(S(abs_done), 1)
                link(dve.tensor_scalar(t[5][:], t[0][:], 0.0, None, ALU.max))

            def softplus_ratio(t, exp_done):
                dve.wait_ge(S(exp_done), 1)
                e = t[2]
                link(dve.tensor_scalar(t[1][:], e[:], 2.0, None, ALU.add))
                link(dve.reciprocal(t[3][:], t[1][:]))
                link(dve.tensor_tensor(t[4][:], e[:], t[3][:], ALU.mult))
                link(dve.tensor_tensor(t[1][:], t[4][:], t[4][:], ALU.mult))

            def softplus_series(t):
                link(dve.tensor_scalar(t[3][:], t[1][:], 1.0 / (2 * LOG1P_TERMS + 1), None, ALU.mult))
                for n in range(LOG1P_TERMS - 1, 0, -1):
                    link(dve.scalar_tensor_tensor(out=t[3][:], in0=t[3][:], scalar=1.0 / (2 * n + 1), in1=t[1][:],
                                                  op0=ALU.add, op1=ALU.mult))
                link(dve.scalar_tensor_tensor(out=t[3][:], in0=t[3][:], scalar=1.0, in1=t[4][:],
                                              op0=ALU.add, op1=ALU.mult))
                link(dve.scalar_tensor_tensor(out=t[3][:], in0=t[3][:], scalar=2.0, in1=t[5][:],
                                              op0=ALU.mult, op1=ALU.add))

            def scores_max(n, s):
                for m in range(2):
                    dve.wait_ge(S("s"), 8 * n + 2 * s + m + 10)
                    dve.tensor_reduce(negmax[:, s % 2, m:m + 1], SB[m][:, 0:(s + 1) * P], AX.X, ALU.max,
                                      negate=True).then_inc(S("max"), 1)

            def normalise(k, u, s):
                n, N = 2 * u + (k == "d"), (s + 1) * P
                p0, p1 = (pr[s % 2][m][:, 0:N] for m in range(2))
                r0, r1 = (rinv[:, s % 2, m:m + 1] for m in range(2))
                dve.wait_ge(S("exp"), 8 * n + 2 * s + 4)
                dve.reciprocal(rinv[:, s % 2, :], rowsum[:, s % 2, :]).then_inc(S("rinv"), 1)
                dve.wait_ge(S("rinv"), 4 * n + s + 1)
                if k == "f":
                    dve.tensor_scalar(p0, p0, r0, None, ALU.mult)
                    dve.tensor_scalar(p1, p1, r1, None, ALU.mult).then_inc(S("p"), 1)
                else:
                    dve.tensor_scalar(p1, p1, r1, neglam[:, 0:1], ALU.mult, ALU.mult).then_inc(S("p1"), 1)
                    dve.wait_ge(S("p1"), 4 * u + s + 1)
                    dve.scalar_tensor_tensor(out=p0, in0=p0, scalar=r0, in1=p1, op0=ALU.mult,
                                             op1=ALU.add).then_inc(S("p"), 1)

            def p_lo(k, n, s):
                N = (s + 1) * P
                dve.wait_ge(S("pT_hi"), 4 * n + s + 1)
                for m in range(2 if k == "f" else 1):
                    last = dve.tensor_tensor(pt[m][1][:, 0:N], TB[m][:, 0:N], pt[m][0][:, 0:N].bitcast(F32),
                                             ALU.subtract)
                last.then_inc(S("pT_lo"), 1)

            def v_out(n, T, bank_):
                dve.wait_ge(S("tile_done"), T + 3)
                dve.wait_ge(S("v_turned"), n + 1)
                dve.tensor_tensor(vt[:], bank_[:], rb[:], ALU.mult).then_inc(S("g_out"), 1)

            def v_lo_part(k, n):
                dve.wait_ge(S("v_hi"), n + 1)
                turned = XB[:].rearrange("p (b d) -> p b d", d=P)
                if k == "f":
                    for m in range(2):
                        half = slice(HD * m, HD * (m + 1))
                        last = dve.tensor_tensor(vs[k][m][1][:, :, half], turned[:, :, half],
                                                 vs[k][m][0][:, :, half].bitcast(F32), ALU.subtract)
                else:
                    last = dve.tensor_tensor(vs[k][0][1][:], turned, vs[k][0][0][:].bitcast(F32), ALU.subtract)
                last.then_inc(S("v_lo"), 1)

            def qk_out(n, r, T, bank_):
                dve.wait_ge(S("tile_done"), T + 3)
                dve.wait_ge(S("qk"[r] + "_lo"), n + 1)
                dve.scalar_tensor_tensor(out=ev[r][:], in0=bank_[:], scalar=(HD ** -0.5, 1.0)[r], in1=rb[:],
                                         op0=ALU.mult, op1=ALU.mult).then_inc(S("g_out"), 1)

            def rope_cos(u, r, T):
                dve.wait_ge(S("g_out"), T + 3)
                dve.wait_ge(S("rope"), 2 * u + r + 1)
                dve.tensor_tensor(rot[:], ev[r][:], cos[:], ALU.mult).then_inc(S("rope_a"), 1)

            def rope_sin(u, r):
                dve.wait_ge(S("swapped"), 2 * u + r + 1)
                dve.tensor_tensor(sw[:], sw[:], sin[:], ALU.mult).then_inc(S("rope_b"), 1)
                dve.wait_ge(S("rope_a"), 2 * u + r + 1)
                dve.wait_ge(S("rope_b"), 2 * u + r + 2)
                dve.tensor_tensor(ev[r][:], rot[:], sw[:], ALU.add).then_inc(S("rope"), 1)

            def qk_lo_part(k, n, r):
                dve.wait_ge(S("qk"[r] + "_hi"), n + 1)
                t = (qs, ks)[r][k]
                dve.tensor_tensor(t[1][:], ev[r][:], t[0][:].bitcast(F32), ALU.subtract)\
                    .then_inc(S("qk"[r] + "_lo"), 1)

            def out_lo(k, u, n):
                if k == "f":
                    dve.wait_ge(S("y_hi"), n + 1)
                    dve.tensor_tensor(columns(yT[1], u), OB[:], columns(yT[0], u).bitcast(F32), ALU.subtract)\
                        .then_inc(S("o_out"), 1)
                    return
                dve.wait_ge(S("d_rs"), u + 1)
                dve.wait_ge(S("dy_lo"), u + 1)
                dve.scalar_tensor_tensor(out=dy[:], in0=OB[:], scalar=sublnw[:, 0:1], in1=drs[:], op0=ALU.mult,
                                         op1=ALU.mult).then_inc(S("o_out"), 1)
                dve.wait_ge(S("y_hi"), n + 1)
                dve.tensor_tensor(columns(yT[1], u + UNITS), dy[:], columns(yT[0], u + UNITS).bitcast(F32),
                                  ALU.subtract).then_inc(S("dy_lo"), 1)

            def section(att, proj):
                if proj:
                    kp, up = proj
                    np_, j0 = 2 * up + (kp == "d"), 3 * (kp == "d")
                    T0 = T_ATTN + 6 * up + j0

                def v_first():
                    if proj:
                        v_out(np_, T0, GB[j0 % 2])

                def qk_first(r):
                    if proj:
                        qk_out(np_, r, T0 + 1 + r, GB[(j0 + 1 + r) % 2])
                        if kp == "d":
                            rope_cos(up, r, T0 + 1 + r)

                def qk_turn(r):
                    if proj and kp == "d":
                        rope_sin(up, r)

                def qk_lo(r):
                    if proj:
                        qk_lo_part(kp, np_, r)
                k, u = att
                n = 2 * u + (k == "d")
                scores_max(n, 0)
                normalise(k, u, 0)
                v_first()
                scores_max(n, 1)
                p_lo(k, n, 0)
                normalise(k, u, 1)
                scores_max(n, 2)
                if proj:
                    v_lo_part(kp, np_)
                p_lo(k, n, 1)
                qk_first(0)
                normalise(k, u, 2)
                scores_max(n, 3)
                qk_turn(0)
                p_lo(k, n, 2)
                qk_lo(0)
                normalise(k, u, 3)
                p_lo(k, n, 3)
                qk_first(1)
                qk_turn(1)
                qk_lo(1)
                out_lo(k, u, n)

            dve.wait_ge(S("rb"), 1)
            dve.wait_ge(S("ff_mm"), 1)
            link(dve.tensor_tensor(ff_t[1][:], OB[0:FOX_HEADS, :], rb[0:FOX_HEADS, :], ALU.mult))
            link(dve.tensor_scalar(ff_t[0][:], ff_t[1][:], bff[:, 0:1], -1.0, ALU.add, ALU.mult))
            softplus_abs(ff_t, "ff_abs")
            v_out(0, T_ATTN, GB[0])
            softplus_ratio(ff_t, "ff_exp")
            qk_out(0, 0, T_ATTN + 1, GB[1])
            softplus_series(ff_t)
            qk_out(0, 1, T_ATTN + 2, GB[0])
            link(dve.tensor_tensor_scan(ff_t[4][:], ff_ones[:], ff_t[3][:], 0.0, ALU.mult, ALU.add))
            dve.tensor_copy(ff_c[0][:], ff_t[4][:]).then_inc(S("ff_rows"), 1)
            dve.wait_ge(S("ff_rows"), 1)
            dve.tensor_tensor(ff_c[1][:], ff_t[4][:], ff_c[0][:].bitcast(F32), ALU.subtract).then_inc(S("ff_rows"), 1)
            qk_lo_part("f", 0, 0)
            v_lo_part("f", 0)
            qk_lo_part("f", 0, 1)

            with dve.Fori(0, UNITS - 1) as i:
                section(("f", i), ("d", i))
                section(("d", i), ("f", i + 1))
            section(("f", UNITS - 1), ("d", UNITS - 1))
            section(("d", UNITS - 1), None)

            def residual(T, R, c, n, bank_, keep=True):
                dve.wait_ge(S("tile_done"), T + 3)
                dve.tensor_tensor(columns(x, c), columns(x, c), bank_[:], ALU.add).then_inc(S("x_add"), 1)

            dve.wait_ge(S("ms"), 1)
            dve.memset(acc[:], 0.0).then_inc(S("setup"), 1)
            dve.wait_ge(S("setup"), 7)
            with dve.Fori(0, KC // 2) as i:
                for j in range(2):
                    residual(T_AO + 2 * i + j, RES_AO + 2 * i + j, 2 * i + j, 1, GB[j])
                    dve.wait_ge(S("x_add"), RES_AO - KC + 2 * i + j + 1)
                    dve.nop().then_inc(S("g_out"), 1)
                    x_chunk(RES_AO + 2 * i + j, 2 * i + j, 1)

            def ffn(l, R, norm, adds):
                with dve.Fori(0, FC) as i:
                    n, T = FC * l + i, T_GU[l] + 2 * i
                    dve.wait_ge(S("rb"), norm)
                    dve.wait_ge(S("tile_done"), T + 3)
                    dve.wait_ge(S("ffn_silu"), n + 1)
                    dve.scalar_tensor_tensor(out=fz[:], in0=GB[0][:], scalar=0.5, in1=rb[:], op0=ALU.mult,
                                             op1=ALU.mult).then_inc(S("ffn_z"), 1)
                    dve.wait_ge(S("ffn_z"), n + 1)
                    dve.nop().then_inc(S("g_out"), 1)
                    dve.wait_ge(S("ffn_tanh"), n + 1)
                    dve.scalar_tensor_tensor(out=fs[:], in0=ft[:], scalar=1.0, in1=fz[:], op0=ALU.add,
                                             op1=ALU.mult).then_inc(S("ffn_silu"), 1)
                    dve.wait_ge(S("tile_done"), T + 4)
                    dve.tensor_tensor(fu[:], GB[1][:], rb[:], ALU.mult).then_inc(S("g_out"), 1)
                    dve.wait_ge(S("ffn_silu"), n + 2)
                    dve.wait_ge(S("g_out"), G_GU[l] + 2 * i + 4)
                    dve.tensor_tensor(fa[:], fs[:], fu[:], ALU.mult).then_inc(S("ffn_act"), 1)
                    dve.wait_ge(S("act_hi"), n + 1)
                    dve.tensor_tensor(columns(act[1], i), fa[:], columns(act[0], i).bitcast(F32), ALU.subtract)\
                        .then_inc(S("act_lo"), 1)
                last = l == 1
                if l == 0:
                    dve.wait_ge(S("dt_w_hi"), 1)
                    dve.tensor_tensor(first_columns(dt_w[2], SSM_HEADS), dt_w[0][:],
                                      first_columns(dt_w[1], SSM_HEADS).bitcast(F32), ALU.subtract)\
                        .then_inc(S("dt_w_lo"), 1)
                link(dve.memset(acc[:], 0.0))
                with dve.Fori(0, KC // 2) as i:
                    for m in range(2):
                        residual(T_DN[l] + 6 * i + 3 * m + 2, R + 2 * i + m, 2 * i + m, norm, GB[m])
                        dve.wait_ge(S("x_add"), R - KC + 2 * i + m + 1)
                        dve.nop().then_inc(S("g_out"), 1)
                        x_chunk(R + 2 * i + m, 2 * i + m, norm, not last)

            dve.nop().then_inc(S("ffn_silu"), 1)
            ffn(0, RES_DN0, 2, 0)

            CB, TR, STB, YD, YO, NX = SB[0], SB[1], TB[0], TB[1], OB, XB

            def u_out(g, j):
                dve.wait_ge(S("tile_done"), T_SSM + 6 * g + j + 3)
                if j < 4:
                    dve.wait_ge(S("conv"), 12 * g + 1)
                    dve.tensor_tensor(ub[j][:, 3:], GB[j % 2][:], rb[:], ALU.mult).then_inc(S("g_out"), 1)
                else:
                    dve.wait_ge(S("gated"), 2 * g + j - 3)
                    dve.scalar_tensor_tensor(out=zc[j - 4][:], in0=GB[j % 2][:], scalar=0.5, in1=rb[:],
                                             op0=ALU.mult, op1=ALU.mult).then_inc(S("g_out"), 1)

            def par(g, n):
                return columns(gp, g * GPW + n, 1)

            def conv(g, j):
                n = 12 * g + 3 * j
                dve.wait_ge(S("conv_first"), 4 * g + j + 1)
                for k in range(3):
                    if k > 0:
                        dve.wait_ge(S("conv"), n + k + 1)
                    dve.scalar_tensor_tensor(out=xs[j][:], in0=ub[j][:, k:k + SEQ], scalar=par(g, 5 * j + k),
                                             in1=xs[j][:], op0=ALU.mult, op1=ALU.add).then_inc(S("conv"), 1)

            def silu(n, t, par_):
                dve.wait_ge(S("tanh"), n + 1)
                dve.scalar_tensor_tensor(out=t[:], in0=tt[par_][:], scalar=1.0, in1=t[:], op0=ALU.add,
                                         op1=ALU.mult).then_inc(S("silu"), 1)

            def sub_lo(lo, src, hi):
                return dve.tensor_tensor(lo, src, hi.bitcast(F32), ALU.subtract)

            def bc_lo(g, j):
                dve.wait_ge(S("bc_hi"), 2 * g + j + 1)
                dve.tensor_tensor(bc[j][1][:], xs[2 + j][:], bc[j][0][:].bitcast(F32), ALU.subtract)\
                    .then_inc(S("bc_lo"), 1)

            for name, credit in (("silu", 2), ("conv", 1), ("cb_masked", 1), ("y_sum", 1), ("state_out", 1),
                                 ("gated", 2), ("g_norm", 1), ("bc_lo", 1), ("m", 1)):
                dve.nop().then_inc(S(name), credit)
            link(dve.tensor_scalar(gp[:].rearrange("p (g n) -> p g n", n=GPW)[:, :, 0:20],
                                   gp[:].rearrange("p (g n) -> p g n", n=GPW)[:, :, 0:20], 0.5, None, ALU.mult))
            for j in range(4):
                dve.memset(ub[j][:, 0:3], 0.0)
            for r in range(HPG):
                for part in range(2):
                    last = dve.memset(xp[r][part][:, :, HD * (1 - r % 2):HD * (2 - r % 2)].bitcast(F32), 0.0)
            link(last)
            dve.wait_ge(S("rb"), 3)
            dve.wait_ge(S("dt_mm"), 1)
            link(dve.tensor_tensor(dt_t[1][:], CB[0:SSM_HEADS, :], rb[0:SSM_HEADS, :], ALU.mult))
            link(dve.tensor_scalar(dt_t[0][:], dt_t[1][:], hp[:, 0:1], None, ALU.add))
            softplus_abs(dt_t, "dt_abs")
            u_out(0, 0)
            softplus_ratio(dt_t, "dt_exp")
            u_out(0, 1)
            conv(0, 0)
            softplus_series(dt_t)
            dve.wait_ge(S("A_exp"), 1)
            link(dve.tensor_scalar(dt_t[5][:], dt_t[3][:], acol[:, 0:1], -1.0, ALU.mult, ALU.mult))
            link(dve.memset(dt_t[1][:], 1.0))
            for c in range(NQB):
                cut = slice(c * P, (c + 1) * P)
                last = dve.tensor_tensor_scan(dt_t[4][:, cut], dt_t[1][:, cut], dt_t[5][:, cut], 0.0,
                                              ALU.mult, ALU.add)
            last.then_inc(S("acs"), 1)
            u_out(0, 2)
            silu(0, xs[0], 0)
            conv(0, 1)
            u_out(0, 3)
            silu(1, xs[1], 1)
            dve.wait_ge(S("acs_turned"), 1)
            dve.tensor_copy(acsT[:], TR[:, 0:NH4]).then_inc(S("acs_T"), 1)
            link(dve.tensor_copy(dtT[:], TR[:, NH4:2 * NH4]))
            link(dve.tensor_scalar(nacs[:], TR[:, 0:NH4], -1.0, None, ALU.mult))
            conv(0, 2)
            silu(2, xs[2], 0)
            dve.wait_ge(S("acs_end"), 1)
            dve.wait_ge(S("acs_T"), 1)
            dve.tensor_tensor(decT[:], YD[:, 0:NH4], acsT[:], ALU.subtract).then_inc(S("dec_T"), 1)
            bc_lo(0, 0)
            conv(0, 3)
            u_out(0, 4)
            silu(3, xs[3], 1)
            bc_lo(0, 1)
            u_out(0, 5)
            for t in range(2):
                silu(4 + t, zc[t], t)
            dve.wait_ge(S("decays"), 2)

            def head_cols(t, g, t2, nchunks):
                at = HPG * g + 2 * t2
                v = t[:].rearrange("p (c h) -> p c h", h=SSM_HEADS)
                v = v[:, 0:nchunks, at:at + 2] if isinstance(at, int) else v[:, 0:nchunks, bass.ds(at, 2)]
                return v.unsqueeze(3).broadcast_to([P, nchunks, 2, HD])

            def decay_args(g, r):
                dve.wait_ge(S("ea"), g + 1)
                for c in range(NQB):
                    cut = ab[:, r * SEQ + c * P:r * SEQ + (c + 1) * P]
                    last = dve.tensor_scalar(cut, cut, width_at(nacs, c * SSM_HEADS + HPG * g + r, 1), 0.0,
                                             ALU.add, ALU.min)
                last.then_inc(S("decay_arg"), 1)

            def m_part(g, r):
                dve.wait_ge(S("decay"), HPG * g + r + 1)
                cut = ab[:, r * SEQ:(r + 1) * SEQ]
                dve.tensor_tensor(cut, cut, cbm[:], ALU.mult).then_inc(S("m"), 1)

            def new_state(g, c):
                n = 3 * g + c
                dve.wait_ge(S("state_mm"), 3 * g + max(c, 1) + 2)
                dve.wait_ge(S("state_out"), n + 1)
                src = STB[:, (c % 2) * 2 * P:(c % 2 + 1) * 2 * P]
                if c == 0:
                    dve.tensor_copy(state[0][:], src).then_inc(S("state_out"), 1)
                    return
                if c == 2:
                    dve.wait_ge(S("prev_lo"), n - 1)
                for r in range(HPG):
                    cut = slice(HD * r, HD * (r + 1))
                    last = dve.scalar_tensor_tensor(
                        out=state[c % 2][:, cut], in0=state[(c + 1) % 2][:, cut],
                        scalar=width_at(cdT, c * SSM_HEADS + HPG * g + r, 1), in1=src[:, cut],
                        op0=ALU.mult, op1=ALU.add)
                last.then_inc(S("state_out"), 1)

            def prev_lo(g, c):
                dve.wait_ge(S("prev_hi"), 3 * g + c + 1)
                cut = slice(c * 2 * P, (c + 1) * 2 * P)
                dve.tensor_tensor(prev[1][:, cut], state[c % 2][:], prev[0][:, cut].bitcast(F32), ALU.subtract)\
                    .then_inc(S("prev_lo"), 1)

            def y_within(g, t):
                y = columns(gT, 2 * g + t)
                dve.wait_ge(S("y_diag"), 2 * g + t + 2)
                dve.wait_ge(S("y_part"), 6 * g + 2)
                dve.tensor_tensor(y, y, YD[:], ALU.add).then_inc(S("y_part"), 1)

            def y_sum(g, t):
                y_late = width_at(gT, (2 * g + t) * SEQ + P, SEQ - P)
                dve.wait_ge(S("y_off"), 2 * g + t + 3)
                dve.wait_ge(S("ea"), g + 1)
                dve.tensor_tensor(ea[t][:, P:], YO[:, P:], ea[t][:, P:], ALU.mult).then_inc(S("y_part"), 1)
                dve.wait_ge(S("y_part"), 6 * g + 2 * t + 4)
                dve.tensor_tensor(y_late, y_late, ea[t][:, P:], ALU.add).then_inc(S("y_sum"), 1)

            def gate(g, t):
                dve.wait_ge(S("y_sum"), 2 * g + t + 2)
                dve.wait_ge(S("silu"), 6 * g + 8)
                y = columns(gT, 2 * g + t)
                dve.tensor_tensor(y, y, zc[t][:], ALU.mult).then_inc(S("gated"), 1)

            def norm_out(g):
                dve.wait_ge(S("rg"), g + 1)
                for t in range(2):
                    dve.scalar_tensor_tensor(out=columns(gT, 2 * g + t), in0=columns(gT, 2 * g + t),
                                             scalar=par(g, 22 + t), in1=rg[:], op0=ALU.mult,
                                             op1=ALU.mult).then_inc(S("g_norm"), 1)

            def ssm_section(g, ahead):
                def uf(j):
                    if ahead is not None:
                        u_out(ahead, j)

                def cf(j):
                    if ahead is not None:
                        conv(ahead, j)

                def sf(j):
                    if ahead is not None:
                        silu(6 * ahead + j, xs[j], j % 2)
                for t in range(2):
                    dve.tensor_scalar(columns(gT, 2 * g + t), xs[t][:], par(g, 20 + t), None, ALU.mult)\
                        .then_inc(S("y_part"), 1)
                decay_args(g, 0)
                decay_args(g, 1)
                uf(0)
                dve.wait_ge(S("cb"), g + 1)
                dve.wait_ge(S("m"), HPG * g + 1)
                dve.tensor_tensor(cbm[:].rearrange("p (c l) -> p c l", l=P), CB[:].rearrange("p (c l) -> p c l", l=P),
                                  causal[:].unsqueeze(1).broadcast_to([P, NQB, P]), ALU.mult)\
                    .then_inc(S("cb_masked"), 1)
                dve.wait_ge(S("xd_lo"), g + 1)
                for t, b in enumerate((TR, YD)):
                    dve.wait_ge(S(f"x{t}_turned"), g + 1)
                    last = dve.tensor_tensor(
                        xst[:, :, t * P:(t + 1) * P].rearrange("p c (h d) -> p c h d", d=HD),
                        b[:].rearrange("p (c h d) -> p c h d", h=2, d=HD), head_cols(dtT, g, t, NQB), ALU.mult)
                last.then_inc(S("x_dt"), 1)
                dve.wait_ge(S("cb_masked"), g + 2)
                m_part(g, 0)
                dve.wait_ge(S("bt_hi"), g + 1)
                dve.tensor_tensor(bt[1][:], YO[:, 0:3 * P], bt[0][:].bitcast(F32), ALU.subtract)\
                    .then_inc(S("bt_lo"), 1)
                dve.wait_ge(S("xp_hi"), g + 1)
                for r in range(HPG):
                    half = slice(HD * (r % 2), HD * (r % 2 + 1))
                    last = dve.tensor_tensor(xp[r][1][:, :, half], xst[:, :, HD * r:HD * (r + 1)],
                                             xp[r][0][:, :, half].bitcast(F32), ALU.subtract)
                last.then_inc(S("xp_lo"), 1)
                dve.wait_ge(S("xp_lo"), g + 1)
                for t in range(2):
                    cut = xst[:, 0:3, t * P:(t + 1) * P].rearrange("p c (h d) -> p c h d", d=HD)
                    last = dve.tensor_tensor(cut, cut, head_cols(dsT, g, t, 3), ALU.mult)
                last.then_inc(S("x_decayed"), 1)
                m_part(g, 1)
                uf(1)
                dve.wait_ge(S("xd_hi"), g + 1)
                dve.tensor_tensor(xd[1][:], xst[:, 0:3, :], xd[0][:].bitcast(F32), ALU.subtract)\
                    .then_inc(S("xd_lo"), 1)
                decay_args(g, 2)
                decay_args(g, 3)
                new_state(g, 0)
                new_state(g, 1)
                cf(0)
                prev_lo(g, 0)
                prev_lo(g, 1)
                uf(2)
                new_state(g, 2)
                m_part(g, 2)
                m_part(g, 3)
                prev_lo(g, 2)
                sf(0)
                if not (isinstance(g, int) and g == 0):
                    norm_out(g - 1)
                y_within(g, 0)
                cf(1)
                y_sum(g, 0)
                gate(g, 0)
                uf(3)
                sf(1)
                cf(2)
                y_within(g, 1)
                sf(2)
                y_sum(g, 1)
                gate(g, 1)
                uf(4)
                if ahead is not None:
                    bc_lo(ahead, 0)
                cf(3)
                sf(3)
                if ahead is not None:
                    bc_lo(ahead, 1)
                uf(5)
                if ahead is not None:
                    for t in range(2):
                        silu(6 * ahead + 4 + t, zc[t], t)

            dve.nop().then_inc(S("xd_lo"), 1)
            ssm_section(0, 1)
            with dve.Fori(1, GROUPS - 1) as g:
                ssm_section(g, g + 1)
            ssm_section(GROUPS - 1, None)
            norm_out(GROUPS - 1)

            dve.wait_ge(S("g_norm"), 2 * GROUPS + 1)
            for n, c in enumerate((*range(KC, 2 * KC), *range(KC))):
                dve.wait_ge(S("gs_hi"), n + 1)
                sub_lo(columns(gs[1], c), columns(gT, c), columns(gs[0], c)).then_inc(S("gs_lo"), 1)
            dve.wait_ge(S("g_ms"), GROUPS + 1)
            dve.memset(acc[:], 0.0).then_inc(S("setup"), 1)
            dve.wait_ge(S("setup"), 8)
            with dve.Fori(0, KC // 2) as i:
                for m in range(2):
                    residual(T_SO + 4 * i + 2 + m, RES_SO + 2 * i + m, 2 * i + m, 3, GB[m])
                    dve.wait_ge(S("x_add"), RES_SO - KC + 2 * i + m + 1)
                    dve.nop().then_inc(S("g_out"), 1)
                    x_chunk(RES_SO + 2 * i + m, 2 * i + m, 3)

            ffn(1, RES_DN1, 4, 0)

            last_norm(dve, LAST_DVE, "y_out")


def kernel(**inputs):
    import concourse.bacc as bacc
    from concourse.bass_utils import run_bass_kernel_spmd

    a = {k: np.asarray(v) for k, v in inputs.items()}

    def tiles(w, starts, pad=P):
        K = w.shape[0]
        return [w[:, c:c + P].reshape(K // P, P, P).transpose(1, 0, 2).reshape(P, K) for c in starts]

    wi = a["attn_w_in"][0]
    FW = FOX_HEADS * HD
    off = {"fq": 0, "fk": FW, "fv": 2 * FW, "ff": 3 * FW, "dq": 3 * FW + FOX_HEADS}
    off["dk"] = off["dq"] + FW
    off["dv"] = off["dk"] + FW
    arrays = {}
    arrays["xT"] = a["x"][0].T.reshape(KC, P, SEQ)
    arrays["w_ff"] = wi[:, off["ff"]:off["ff"] + FOX_HEADS].reshape(KC, P, FOX_HEADS).transpose(1, 0, 2)
    arrays["w_attn"] = np.concatenate(tiles(wi, [off[k + r] + P * u for u in range(UNITS) for k in "fd" for r in "vqk"]))
    arrays["w_ao"] = np.concatenate(tiles(a["attn_w_out"][0], range(0, DM, P)))
    gu = [np.concatenate([t for g, u in zip(tiles(a["ffn_w_gate"][l], range(0, DFF, P)),
                                            tiles(a["ffn_w_up"][l], range(0, DFF, P))) for t in (g, u)])
          for l in range(2)]
    arrays["w_gu"] = np.stack(gu)
    arrays["w_dn"] = np.stack([np.concatenate(tiles(a["ffn_w_down"][l], range(0, DM, P))) for l in range(2)])
    SP_ = a["ssm_w_in"][0]
    conv_dim = DI + 2 * GROUPS * P
    arrays["w_dt"] = SP_[:, DI + conv_dim:].reshape(KC, P, SSM_HEADS).transpose(1, 0, 2)
    xoff, boff, coff = DI, 2 * DI, 2 * DI + GROUPS * P
    arrays["w_ssm"] = np.concatenate(tiles(SP_, [o for g in range(GROUPS) for o in (
        xoff + 2 * P * g, xoff + 2 * P * g + P, boff + P * g, coff + P * g, 2 * P * g, 2 * P * g + P)]))
    arrays["w_so"] = np.concatenate(tiles(a["ssm_w_out"][0], range(0, DM, P)))
    arrays["ssm_heads"] = np.stack([a["ssm_dt_bias"][0], a["ssm_a_log"][0]], 1)
    taps = np.concatenate([a["ssm_conv_w"][0], a["ssm_conv_b"]]).reshape(5, 4 * GROUPS, P)
    d = np.repeat(a["ssm_d"][0], HD).reshape(2 * GROUPS, P)
    nw = a["ssm_norm"][0].reshape(2 * GROUPS, P)
    rows = []
    for g in range(GROUPS):
        for t in (2 * g, 2 * g + 1, 2 * GROUPS + g, 3 * GROUPS + g):
            rows += [taps[n, t] for n in range(5)]
        rows += [d[2 * g], d[2 * g + 1], nw[2 * g], nw[2 * g + 1]]
    arrays["ssm_params"] = np.stack(rows, 1)
    norms = [a["norm_mix"][0], a["norm_ffn"][0], a["norm_mix"][1], a["norm_ffn"][1], a["final_norm"]]
    arrays["gains"] = np.stack([n.reshape(KC, P).T for n in norms], 1).reshape(P, 5 * KC)
    arrays["fox_cols"] = a["attn_b_forget"][0].reshape(FOX_HEADS, 1)
    inv = np.float32(10000.0) ** (-np.arange(0, HD, 2, dtype=np.float32) / np.float32(HD))
    ang = np.arange(SEQ, dtype=np.float32)[:, None] * inv[None, :].astype(np.float32)
    c, s = np.cos(ang).T.astype(np.float32), np.sin(ang).T.astype(np.float32)
    arrays["rope"] = np.stack([np.concatenate([c] * 4), np.concatenate([-s, s] * 2)])
    arrays["lam"] = a["diff_lambda"][0]
    arrays["subln"] = a["diff_subln"][0].reshape(P, 1)
    arrays = {k: np.ascontiguousarray(v) for k, v in arrays.items()}

    nc = bacc.Bacc("TRN2", target_bir_lowering=False, num_devices=1)
    aps = {k: nc.dram_tensor("in_" + k, v.shape, F32, kind="ExternalInput").ap() for k, v in arrays.items()}
    aps["outT"] = nc.dram_tensor("outT", (KC, P, SEQ), F32, kind="ExternalOutput").ap()
    trunk(nc, **aps)
    r = run_bass_kernel_spmd(nc, [{"in_" + k: v for k, v in arrays.items()}], core_ids=[0])
    return np.ascontiguousarray(r.results[0]["outT"].reshape(DM, SEQ).T).reshape(1, SEQ, DM)
```
